# Optimizing a Trainium2 kernel written in Bass

```python
import jax, jax.numpy as jnp
from jax import lax
import numpy as np

D_MODEL = 1024
BATCH = 1
SEQ = 1024
DEPTH = 1

N_MIXERS = 3
CHUNK = 64
Q_BLOCK = 128
HEAD_DIM = 64
N_HEADS = D_MODEL // HEAD_DIM
SWA_KV_HEADS = 4
SWA_GROUP = N_HEADS // SWA_KV_HEADS
SWA_WINDOW = 128
SWA_WIN_CHUNKS = SWA_WINDOW // CHUNK
D_FF = 2816
NORM_EPS = 1e-6
N_FOX = (DEPTH + N_MIXERS - 1) // N_MIXERS
N_SB = (DEPTH + N_MIXERS - 2) // N_MIXERS
N_SWA = (DEPTH + N_MIXERS - 3) // N_MIXERS

kernel_name = "chunk_causal_hybrid_fox_stickbreak_swa_macaron"

def rms_norm(x, g):
    xf = x.astype(jnp.float32)
    y = xf * lax.rsqrt(jnp.mean(xf * xf, axis=-1, keepdims=True) + NORM_EPS)
    return (y * g.astype(jnp.float32)).astype(x.dtype)

def swiglu(x, w_gate, w_up, w_down):
    return (jax.nn.silu(x @ w_gate) * (x @ w_up)) @ w_down

def to_blocks(a):
    b, s = a.shape[:2]
    a = a.reshape((b, s // Q_BLOCK, Q_BLOCK) + a.shape[2:])
    return jnp.moveaxis(a, 1, 0)

def from_blocks(a):
    a = jnp.moveaxis(a, 0, 1)
    return a.reshape((a.shape[0], a.shape[1] * a.shape[2]) + a.shape[3:])

def forgetting_attention(h, w_in, b_f, w_o):
    b, s, _ = h.shape
    scale = HEAD_DIM ** -0.5
    q, k, v, f_logit = jnp.split(h @ w_in, [D_MODEL, 2 * D_MODEL, 3 * D_MODEL], axis=-1)
    q = q.reshape(b, s, N_HEADS, HEAD_DIM)
    k = k.reshape(b, s, N_HEADS, HEAD_DIM)
    v = v.reshape(b, s, N_HEADS, HEAD_DIM)
    log_f = jax.nn.log_sigmoid((f_logit + b_f).astype(jnp.float32))
    cum = jnp.cumsum(log_f, axis=1)
    cum_k = jnp.moveaxis(cum, 1, 2)[:, :, None, :]
    key_pos = jnp.arange(s)

    def block(args):
        qb, fq, t0 = args
        sc = jnp.einsum('bqhd,bkhd->bhqk', qb, k, preferred_element_type=jnp.float32) * scale
        sc = sc + jnp.moveaxis(fq, 1, 2)[..., None] - cum_k
        q_pos = t0 + jnp.arange(Q_BLOCK)
        causal = key_pos[None, :] <= q_pos[:, None]
        p = jax.nn.softmax(jnp.where(causal, sc, -jnp.inf), axis=-1)
        return jnp.einsum('bhqk,bkhd->bqhd', p.astype(v.dtype), v)

    starts = jnp.arange(s // Q_BLOCK) * Q_BLOCK
    o = from_blocks(lax.map(block, (to_blocks(q), to_blocks(cum), starts)))
    return o.reshape(b, s, D_MODEL) @ w_o

def stick_breaking_attention(h, w_in, w_o):
    b, s, _ = h.shape
    scale = HEAD_DIM ** -0.5
    q, k, v = jnp.split(h @ w_in, [D_MODEL, 2 * D_MODEL], axis=-1)
    q = q.reshape(b, s, N_HEADS, HEAD_DIM)
    k = k.reshape(b, s, N_HEADS, HEAD_DIM)
    v = v.reshape(b, s, N_HEADS, HEAD_DIM)
    key_pos = jnp.arange(s)

    def block(args):
        qb, t0 = args
        z = jnp.einsum('bqhd,bkhd->bhqk', qb, k, preferred_element_type=jnp.float32) * scale
        q_pos = t0 + jnp.arange(Q_BLOCK)
        strict = key_pos[None, :] < q_pos[:, None]
        log_beta = jax.nn.log_sigmoid(z)
        log_rest = jnp.where(strict, jax.nn.log_sigmoid(-z), 0.0)
        suffix = lax.cumsum(log_rest, axis=3, reverse=True) - log_rest
        a = jnp.where(strict, jnp.exp(log_beta + suffix), 0.0)
        return jnp.einsum('bhqk,bkhd->bqhd', a.astype(v.dtype), v)

    starts = jnp.arange(s // Q_BLOCK) * Q_BLOCK
    o = from_blocks(lax.map(block, (to_blocks(q), starts)))
    return o.reshape(b, s, D_MODEL) @ w_o

def sliding_window_sink_attention(h, w_in, sinks, w_o):
    b, s, _ = h.shape
    nc = s // CHUNK
    scale = HEAD_DIM ** -0.5
    kv_w = SWA_KV_HEADS * HEAD_DIM
    q, k, v = jnp.split(h @ w_in, [D_MODEL, D_MODEL + kv_w], axis=-1)
    q = q.reshape(b, nc, CHUNK, SWA_KV_HEADS, SWA_GROUP, HEAD_DIM)
    k = k.reshape(b, nc, CHUNK, SWA_KV_HEADS, HEAD_DIM)
    v = v.reshape(b, nc, CHUNK, SWA_KV_HEADS, HEAD_DIM)

    def band(a):
        padded = jnp.pad(a, ((0, 0), (SWA_WIN_CHUNKS - 1, 0), (0, 0), (0, 0), (0, 0)))
        return jnp.concatenate([padded[:, w:w + nc] for w in range(SWA_WIN_CHUNKS)], axis=2)

    kb, vb = band(k), band(v)
    wc = SWA_WIN_CHUNKS * CHUNK
    sc = jnp.einsum('bnqkgd,bnjkd->bnkgqj', q, kb, preferred_element_type=jnp.float32) * scale
    slopes = jnp.exp2(-8.0 * jnp.arange(1, N_HEADS + 1, dtype=jnp.float32) / N_HEADS)
    slopes = slopes.reshape(SWA_KV_HEADS, SWA_GROUP)
    i_idx = jnp.arange(CHUNK, dtype=jnp.float32)[:, None]
    j_idx = jnp.arange(wc, dtype=jnp.float32)[None, :]
    dist = jnp.abs(i_idx - j_idx + (SWA_WIN_CHUNKS - 1) * CHUNK)
    sc = sc - slopes[:, :, None, None] * dist
    valid = (jnp.arange(nc)[:, None] + jnp.arange(wc)[None, :] // CHUNK) >= SWA_WIN_CHUNKS - 1
    sc = jnp.where(valid[None, :, None, None, None, :], sc, -jnp.inf)
    sink = jnp.broadcast_to(sinks.astype(jnp.float32).reshape(SWA_KV_HEADS, SWA_GROUP)[:, :, None, None],
                            sc.shape[:-1] + (1,))
    p = jax.nn.softmax(jnp.concatenate([sc, sink], axis=-1), axis=-1)[..., :-1]
    o = jnp.einsum('bnkgqj,bnjkd->bnqkgd', p.astype(vb.dtype), vb)
    return o.reshape(b, s, D_MODEL) @ w_o

def setup_inputs(seed: int = 0) -> dict:
    key = jax.random.key(seed)
    ks = jax.random.split(key, 20)
    f32 = jnp.float32
    dsc = D_MODEL ** -0.5
    fsc = D_FF ** -0.5

    def nrm(k, shape, sc):
        return jax.random.normal(k, shape, f32) * sc

    return {
        "x": nrm(ks[0], (BATCH, SEQ, D_MODEL), 1.0),
        "norm_ffn1": 1.0 + nrm(ks[1], (DEPTH, D_MODEL), 0.02),
        "norm_mix": 1.0 + nrm(ks[2], (DEPTH, D_MODEL), 0.02),
        "norm_ffn2": 1.0 + nrm(ks[3], (DEPTH, D_MODEL), 0.02),
        "norm_final": 1.0 + nrm(ks[4], (D_MODEL,), 0.02),
        "ffn1_w_gate": nrm(ks[5], (DEPTH, D_MODEL, D_FF), dsc),
        "ffn1_w_up": nrm(ks[6], (DEPTH, D_MODEL, D_FF), dsc),
        "ffn1_w_down": nrm(ks[7], (DEPTH, D_FF, D_MODEL), fsc),
        "ffn2_w_gate": nrm(ks[8], (DEPTH, D_MODEL, D_FF), dsc),
        "ffn2_w_up": nrm(ks[9], (DEPTH, D_MODEL, D_FF), dsc),
        "ffn2_w_down": nrm(ks[10], (DEPTH, D_FF, D_MODEL), fsc),
        "fox_w_in": nrm(ks[11], (N_FOX, D_MODEL, 3 * D_MODEL + N_HEADS), dsc),
        "fox_b_f": 2.0 + nrm(ks[12], (N_FOX, N_HEADS), 0.1),
        "fox_w_o": nrm(ks[13], (N_FOX, D_MODEL, D_MODEL), dsc),
        "sb_w_in": nrm(ks[14], (N_SB, D_MODEL, 3 * D_MODEL), dsc),
        "sb_w_o": nrm(ks[15], (N_SB, D_MODEL, D_MODEL), dsc),
        "swa_w_in": nrm(ks[16], (N_SWA, D_MODEL, D_MODEL + 2 * SWA_KV_HEADS * HEAD_DIM), dsc),
        "swa_sinks": nrm(ks[17], (N_SWA, N_HEADS), 0.5),
        "swa_w_o": nrm(ks[18], (N_SWA, D_MODEL, D_MODEL), dsc),
    }

def reference(x, norm_ffn1, norm_mix, norm_ffn2, norm_final,
              ffn1_w_gate, ffn1_w_up, ffn1_w_down,
              ffn2_w_gate, ffn2_w_up, ffn2_w_down,
              fox_w_in, fox_b_f, fox_w_o,
              sb_w_in, sb_w_o,
              swa_w_in, swa_sinks, swa_w_o):
    for i in range(DEPTH):
        kind, j = i % N_MIXERS, i // N_MIXERS
        x = x + 0.5 * swiglu(rms_norm(x, norm_ffn1[i]), ffn1_w_gate[i], ffn1_w_up[i], ffn1_w_down[i])
        hn = rms_norm(x, norm_mix[i])
        if kind == 0:
            y = forgetting_attention(hn, fox_w_in[j], fox_b_f[j], fox_w_o[j])
        elif kind == 1:
            y = stick_breaking_attention(hn, sb_w_in[j], sb_w_o[j])
        else:
            y = sliding_window_sink_attention(hn, swa_w_in[j], swa_sinks[j], swa_w_o[j])
        x = x + y
        x = x + 0.5 * swiglu(rms_norm(x, norm_ffn2[i]), ffn2_w_gate[i], ffn2_w_up[i], ffn2_w_down[i])
    return rms_norm(x, norm_final)


_drawn_inputs = setup_inputs


def setup_inputs(seed=0):
    import zlib

    import numpy as np

    out = dict(_drawn_inputs(seed))
    spreads = {}
    factors = {'norm_ffn1': 5.751,
     'norm_mix': 4.925,
     'norm_ffn2': 8.0,
     'norm_final': 2.877,
     'fox_b_f': 3.227}
    for name, (base, spread) in spreads.items():
        noise = np.random.default_rng([zlib.crc32(name.encode()), seed]).standard_normal(out[name].shape)
        drawn = base * np.exp(spread * noise) if base else spread * noise
        out[name] = __import__('jax').numpy.asarray(drawn.astype(out[name].dtype))
    for name, factor in factors.items():
        out[name] = (out[name] * factor).astype(out[name].dtype)
    return out
```

```python
from contextlib import ExitStack

import concourse.bass as bass
from concourse import mybir

ALU = mybir.AluOpType
ACT = mybir.ActivationFunctionType
AX_X = mybir.AxisListType.X
F32 = mybir.dt.float32
F32R = mybir.dt.float32r

P = 128
BANK = 512
KIB = 1024
EPS = 1e-6


def build(nc, x, norm_ffn1, norm_mix, norm_ffn2, norm_final,
          ffn1_w_gate, ffn1_w_up, ffn1_w_down, ffn2_w_gate, ffn2_w_up, ffn2_w_down,
          fox_w_in, fox_b_f, fox_w_o, out):
    _, S, D = x.shape
    F = ffn1_w_gate.shape[2]
    KT = D // P
    NS = S // BANK
    SB = S // P
    FC = 2 * P
    CHUNKS = F // FC
    assert F % FC == 0 and KT == 8 and NS == 2 and CHUNKS >= 3
    UNITS = 6
    RAW = 3
    STEPS = 2 * NS
    OUTS = NS * KT
    NH = fox_b_f.shape[1]
    HD = D // NH
    PAIRS = NH // 2
    assert HD == 64 and PAIRS == KT and S == 1024

    ctx = ExitStack()
    with ctx:
        def sem(name):
            return ctx.enter_context(nc.semaphore(name))

        arena = ctx.enter_context(nc.sbuf_tensor("arena", [P, 207 * 256], F32))
        base = 16512 if not hasattr(arena, "offset_bytes") else 16512

        def at(name, shape, dt, kib):
            return nc.alloc_sbuf_tensor_at(name, shape, dt, offset=int(base + kib * KIB))

        hn_hi = at("hn_hi", [P, KT, S], F32R, 0)
        hn_lo = at("hn_lo", [P, KT, S], F32R, 32)
        rstd = at("rstd", [P, S], F32, 64)
        raw = at("raw", [P, RAW, 1024], F32, 68)
        wa_hi = at("wa_hi", [P, 3, 1024], F32R, 80)
        wa_lo = at("wa_lo", [P, 3, 1024], F32R, 92)
        ident = at("ident", [P, P], F32, 104)
        ones = at("ones", [P, P], F32R, 104.5)
        gain_rows = at("gain_rows", [4 * KT, P], F32, 105)
        gains = at("gains", [P, 4 * KT], F32, 105.5)
        xT = at("xT", [P, KT, S], F32, 106)
        wb_hi = at("wb_hi", [P, 3, 1024], F32R, 138)
        wb_lo = at("wb_lo", [P, 3, 1024], F32R, 150)
        hid_hi = at("hid_hi", [P, 2, S], F32R, 162)
        hid_lo = at("hid_lo", [P, 2, S], F32R, 170)
        gs = at("gs", [P, 2, BANK], F32, 178)
        us = at("us", [P, 2, BANK], F32, 182)
        sq = at("sq", [P, 2, BANK], F32, 186)
        ssum = at("ssum", [P, NS, BANK], F32, 190)
        ssum_hi = at("ssum_hi", [P, NS, BANK], F32R, 194)
        ssum_lo = at("ssum_lo", [P, NS, BANK], F32R, 198)
        xin = at("xin", [P, 4, D], F32, 162)
        y = at("y", [P, KT, BANK], F32, 0)
        yout = at("yout", [P, 2, D], F32, 32)

        k_parts = at("k_parts", [P, 2, S], F32R, 106)
        k_ext = at("k_ext", [P, 2, S], F32R, 114)
        q_parts = at("q_parts", [P, 2, S], F32R, 122)
        q_ext = at("q_ext", [P, 2, S], F32R, 130)
        t = at("t", [P, 3, S], F32, 138)
        v_parts = at("v_parts", [P, SB, 2, 2, HD], F32R, 150)
        p_low = at("p_low", [P, 4, BANK], F32, 158)
        p_high = at("p_high", [P, 4, S], F32, 166)
        pt_hi = at("pt_hi", [P, 2, BANK], F32R, 182)
        pt_lo = at("pt_lo", [P, 2, BANK], F32R, 186)
        oT = at("oT", [P, S], F32, 190)
        o_half = at("o_half", [P, BANK], F32, 194)
        wo_hi = at("wo_hi", [P, 5, 1024], F32R, 138)
        wo_lo = at("wo_lo", [P, 5, 1024], F32R, 158)
        z = at("z", [NH, S], F32, 158)
        ez = at("ez", [NH, S], F32, 162)
        cum = at("cum", [NH, S], F32, 166)
        ext_rows = at("ext_rows", [NH, 4, S], F32R, 170)
        ident_r = at("ident_r", [P, P], F32R, 202)
        mask = at("mask", [P, P], F32R, 202.5)
        wf_raw = at("wf_raw", [P, KT, NH], F32, 203)
        wf_hi = at("wf_hi", [P, KT, NH], F32R, 203.5)
        wf_lo = at("wf_lo", [P, KT, NH], F32R, 204)
        b_f = at("b_f", [NH, 1], F32, 204.5)
        low = at("low", [P, 16], F32, 204.75)
        rsum = at("rsum", [P, 16], F32, 205)
        rinv = at("rinv", [P, 16], F32, 205.25)
        mask0 = at("mask0", [P, P], F32, 205.5)
        ext_dram = nc.dram_tensor("ext_rows_scratch", [NH, 4, S], F32R, kind="Internal").ap()
        x_dram = nc.dram_tensor("x_scratch", [KT, P, S], F32, kind="Internal").ap()
        o_dram = nc.dram_tensor("o_scratch", [KT, P, S], F32, kind="Internal").ap()

        banks = ctx.enter_context(nc.psum_tensor("banks", [P, 8, BANK], F32))

        def whi(u):
            return wa_hi[:, u, :] if u < 3 else wb_hi[:, u - 3, :]

        def wlo(u):
            return wa_lo[:, u, :] if u < 3 else wb_lo[:, u - 3, :]

        gains_loaded = sem("gains_loaded")
        ident_made = sem("ident_made")
        ones_made = sem("ones_made")
        gains_turned = sem("gains_turned")
        gains_ready = sem("gains_ready")
        x_loaded = [sem(f"x_loaded{i}") for i in range(4)]
        x_turned = sem("x_turned")
        x_kept_act = sem("x_kept_act")
        x_kept_dve = sem("x_kept_dve")

        hn_hi_ready = sem("hn_hi_ready")
        hn_ready = sem("hn_ready")
        sq_ready = sem("sq_ready")
        sq_summed = sem("sq_summed")
        ssum_hi_ready = sem("ssum_hi_ready")
        ssum_ready = sem("ssum_ready")
        stat_ready = sem("stat_ready")
        var_ready = sem("var_ready")
        inv_ready = sem("inv_ready")
        rstd_ready = sem("rstd_ready")
        w_loaded = [sem(f"w_loaded{u}") for u in range(UNITS)]
        w_hi_ready = [sem(f"w_hi_ready{u}") for u in range(UNITS)]
        w_ready = [sem(f"w_ready{u}") for u in range(UNITS)]
        gate_done = sem("gate_done")
        up_done = sem("up_done")
        gate_scaled = sem("gate_scaled")
        up_scaled = sem("up_scaled")
        silu_ready = sem("silu_ready")
        prod_ready = sem("prod_ready")
        hid_hi_ready = sem("hid_hi_ready")
        hid_ready = sem("hid_ready")
        down_done = sem("down_done")
        x_updated = sem("x_updated")

        class Norm:
            def __init__(self, index):
                self.gain = index * KT
                self.tiles = index * NS * KT
                self.halves = index * NS

        class Ffn:
            def __init__(self, start, gate, up, down):
                self.start, self.gate, self.up, self.down = start, gate, up, down

        norm1, norm2, norm3, normf = (Norm(i) for i in range(4))
        ffn1 = Ffn(0, ffn1_w_gate, ffn1_w_up, ffn1_w_down)
        ffn2 = Ffn(CHUNKS, ffn2_w_gate, ffn2_w_up, ffn2_w_down)
        assert KT * NS == OUTS
        gate_in_loaded = sem("gate_in_loaded")
        ident_r_made = sem("ident_r_made")
        mask_made = sem("mask_made")
        wf_hi_ready = sem("wf_hi_ready")
        wf_ready = sem("wf_ready")
        f_done = sem("f_done")
        f_step = sem("f_step")
        f_act = sem("f_act")
        ext_stored = sem("ext_stored")
        x_spilled = sem("x_spilled")
        rows_one = sem("rows_one")
        ext_loaded = [sem(f"ext_loaded{h}") for h in range(2)]
        pw_loaded = [sem(f"pw_loaded{u}") for u in range(3)]
        pw_hi_ready = [sem(f"pw_hi_ready{u}") for u in range(3)]
        pw_ready = [sem(f"pw_ready{u}") for u in range(3)]
        proj_done = sem("proj_done")
        t_ready = sem("t_ready")
        aug_hi_ready = [sem(f"aug_hi_ready{h}") for h in range(2)]
        aug_ready = [sem(f"aug_ready{h}") for h in range(2)]
        scores_done = sem("scores_done")
        low_ready = sem("low_ready")
        exp_ready = sem("exp_ready")
        rinv_ready = sem("rinv_ready")
        p_ready = sem("p_ready")
        turned = sem("turned")
        part_hi_ready = sem("part_hi_ready")
        part_ready = sem("part_ready")
        pv_done = sem("pv_done")
        o_half_ready = sem("o_half_ready")
        o_ready = sem("o_ready")
        oT_free = sem("oT_free")
        tail_loaded = [sem(f"tail_loaded{i}") for i in range(RAW)]
        moved = sem("moved")
        tail_hi_ready = sem("tail_hi_ready")
        tail_ready = sem("tail_ready")
        o7_hi_ready = sem("o7_hi_ready")
        o7_ready = sem("o7_ready")
        x_back = [sem(f"x_back{k}") for k in range(KT)]
        wo_done = sem("wo_done")
        wo_added = sem("wo_added")
        y_ready = sem("y_ready")
        y_turned = sem("y_turned")
        yout_act = sem("yout_act")
        yout_dve = sem("yout_dve")
        stored = [sem(f"stored{i}") for i in range(2)]

        def halves(j):
            n, kt = divmod(j, KT)
            return kt, slice(n * BANK, (n + 1) * BANK)

        def norm_act(norm, j):
            kt, cols = halves(j)
            nc.scalar.activation(hn_hi[:, kt, cols], xT[:, kt, cols], ACT.Copy,
                                 scale=gains[:, norm.gain + kt:norm.gain + kt + 1]).then_inc(hn_hi_ready, 1)

        def square_act(act, norm, j):
            kt, cols = halves(j)
            if j >= 2:
                act.wait_ge(sq_summed, norm.tiles + j - 1)
            nc.scalar.activation(sq[:, j % 2, :], xT[:, kt, cols], ACT.Square).then_inc(sq_ready, 1)

        def norm_dve(dve, norm, j):
            kt, cols = halves(j)
            dve.wait_ge(hn_hi_ready, norm.tiles + j + 1)
            nc.vector.scalar_tensor_tensor(
                out=hn_lo[:, kt, cols], in0=xT[:, kt, cols], scalar=gains[:, norm.gain + kt:norm.gain + kt + 1],
                in1=hn_hi[:, kt, cols].bitcast(F32), op0=ALU.mult, op1=ALU.subtract).then_inc(hn_ready, 1)

        def norm_pool(pool, norm):
            for j in range(NS * KT):
                n, kt = divmod(j, KT)
                pool.wait_ge(sq_ready, norm.tiles + j + 1)
                if kt == 0:
                    nc.gpsimd.tensor_copy(ssum[:, n, :], sq[:, j % 2, :]).then_inc(sq_summed, 1)
                else:
                    pool.wait_ge(sq_summed, norm.tiles + j)
                    nc.gpsimd.tensor_tensor(ssum[:, n, :], ssum[:, n, :], sq[:, j % 2, :],
                                            ALU.add).then_inc(sq_summed, 1)

        def stat_split_act(act, norm, n):
            act.wait_ge(sq_summed, norm.tiles + KT * (n + 1))
            nc.scalar.activation(ssum_hi[:, n, :], ssum[:, n, :], ACT.Copy).then_inc(ssum_hi_ready, 1)

        def stat_split_dve(dve, norm, n):
            dve.wait_ge(ssum_hi_ready, norm.halves + n + 1)
            nc.vector.tensor_tensor(ssum_lo[:, n, :], ssum[:, n, :], ssum_hi[:, n, :].bitcast(F32),
                                    ALU.subtract).then_inc(ssum_ready, 1)

        def stat_pe(pe, norm, n):
            pe.wait_ge(ssum_ready, norm.halves + n + 1)
            nc.tensor.matmul(banks[:, 4 + n, :], ones[:], ssum_hi[:, n, :], start=True, stop=False)
            nc.tensor.matmul(banks[:, 4 + n, :], ones[:], ssum_lo[:, n, :], start=False,
                             stop=True).then_inc(stat_ready, 1)

        def rstd_dve(dve, norm, n):
            cols = slice(n * BANK, (n + 1) * BANK)
            dve.wait_ge(stat_ready, norm.halves + n + 1)
            nc.vector.tensor_scalar(rstd[:, cols], banks[:, 4 + n, :], 1.0 / D, EPS, ALU.mult,
                                    ALU.add).then_inc(var_ready, 1)
            dve.wait_ge(var_ready, norm.halves + n + 1)
            nc.vector.reciprocal(rstd[:, cols], rstd[:, cols]).then_inc(inv_ready, 1)

        def rstd_act(act, norm, n):
            cols = slice(n * BANK, (n + 1) * BANK)
            act.wait_ge(inv_ready, norm.halves + n + 1)
            nc.scalar.activation(rstd[:, cols], rstd[:, cols], ACT.Sqrt).then_inc(rstd_ready, 1)

        def ffn_load(sp, f, c, u):
            at_chunk = (c - f.start) * FC
            dst = raw[:, u % RAW, :]
            if u < 4:
                w = f.gate if u < 2 else f.up
                half = (u % 2) * (D // 2)
                src = w[0, half:half + D // 2, bass.ds(at_chunk, FC)].rearrange("(k p) n -> p k n", p=P)
                dst = dst.rearrange("p (k n) -> p k n", n=FC)
            else:
                src = f.down[0, bass.ds(at_chunk + (u - 4) * P, P), :]
            sp.dma_start(dst, src).then_inc(w_loaded[u], 16)

        def ffn_sync(sp, f):
            for u in range(RAW, UNITS):
                sp.wait_ge(w_ready[u - RAW], f.start + 1)
                ffn_load(sp, f, f.start, u)
            with sp.Fori(f.start + 1, f.start + CHUNKS) as c:
                for u in range(UNITS):
                    if u >= RAW:
                        sp.wait_ge(w_ready[u - RAW], c + 1)
                    else:
                        sp.wait_ge(w_ready[u + RAW], c)
                    ffn_load(sp, f, c, u)

        def w_split_act(act, f, c, u):
            act.wait_ge(w_loaded[u], 16 * (c + 1))
            nc.scalar.activation(whi(u), raw[:, u % RAW, :], ACT.Copy).then_inc(w_hi_ready[u], 1)

        def w_split_dve(dve, f, c, u):
            dve.wait_ge(w_hi_ready[u], c + 1)
            nc.vector.tensor_tensor(wlo(u), raw[:, u % RAW, :], whi(u).bitcast(F32),
                                    ALU.subtract).then_inc(w_ready[u], 1)

        def three(psum, hi, lo, x_hi, x_lo, first, last):
            nc.tensor.matmul(psum, hi, x_lo, start=first, stop=False)
            nc.tensor.matmul(psum, hi, x_hi, start=False, stop=False)
            return nc.tensor.matmul(psum, lo, x_hi, start=False, stop=last)

        def ffn_pe(pe, f, norm, c, first=False):
            for i in range(STEPS):
                t, n = divmod(i, NS)
                cols = slice(n * BANK, (n + 1) * BANK)
                for part, (done, scaled) in enumerate(((gate_done, gate_scaled), (up_done, up_scaled))):
                    psum = banks[:, 2 * (i % 2) + part, :]
                    if i >= 2:
                        pe.wait_ge(scaled, STEPS * c + i - 1)
                    elif i == 0 and not first:
                        pe.wait_ge(scaled, STEPS * c)
                    for k in range(KT):
                        u = 2 * part + k // 4
                        if i == 0 and k % 4 == 0:
                            pe.wait_ge(w_ready[u], c + 1)
                        if first and t == 0 and part == 0:
                            pe.wait_ge(hn_ready, norm.tiles + n * KT + k + 1)
                        w = slice((k % 4) * FC + t * P, (k % 4) * FC + (t + 1) * P)
                        mm = three(psum, whi(u)[:, w], wlo(u)[:, w], hn_hi[:, k, cols], hn_lo[:, k, cols],
                                   k == 0, k == KT - 1)
                    mm.then_inc(done, 1)
                if first and i < NS:
                    stat_pe(pe, norm, i)
            for j in range(OUTS):
                n, m = divmod(j, KT)
                cols = slice(n * BANK, (n + 1) * BANK)
                if j % KT == 0:
                    pe.wait_ge(hid_ready, STEPS * c + 3 + n)
                if j >= 4:
                    pe.wait_ge(x_updated, OUTS * c + j - 3)
                elif j == 0 and not first:
                    pe.wait_ge(x_updated, OUTS * c)
                for t in range(2):
                    if j == 0:
                        pe.wait_ge(w_ready[4 + t], c + 1)
                    w = slice(m * P, (m + 1) * P)
                    mm = three(banks[:, 4 + j % 4, :], whi(4 + t)[:, w], wlo(4 + t)[:, w],
                               hid_hi[:, t, cols], hid_lo[:, t, cols], t == 0, t == 1)
                mm.then_inc(down_done, 1)

        def ffn_act(act, f, norm, c, first=False, last=False):
            for u in (4, 5):
                if not first:
                    act.wait_ge(down_done, OUTS * c)
                w_split_act(act, f, c, u)
            for i in range(STEPS):
                t, n = divmod(i, NS)
                if first and i < NS:
                    rstd_act(act, norm, n)
                act.wait_ge(gate_scaled, STEPS * c + i + 1)
                nc.scalar.activation(gs[:, i % 2, :], gs[:, i % 2, :], ACT.Silu).then_inc(silu_ready, 1)
                act.wait_ge(prod_ready, STEPS * c + i + 1)
                nc.scalar.activation(hid_hi[:, t, n * BANK:(n + 1) * BANK], us[:, i % 2, :],
                                     ACT.Copy).then_inc(hid_hi_ready, 1)
            if not last:
                act.wait_ge(gate_done, STEPS * (c + 1))
                for u in (0, 1):
                    w_split_act(act, f, c + 1, u)
                act.wait_ge(up_done, STEPS * (c + 1))
                for u in (2, 3):
                    w_split_act(act, f, c + 1, u)

        def ffn_dve(dve, f, norm, c, first=False, last=False):
            for u in (4, 5):
                w_split_dve(dve, f, c, u)
            for i in range(STEPS):
                if first and i < NS:
                    rstd_dve(dve, norm, i)
                t, n = divmod(i, NS)
                cols = slice(n * BANK, (n + 1) * BANK)
                b = i % 2
                dve.wait_ge(gate_done, STEPS * c + i + 1)
                if first and i < NS:
                    dve.wait_ge(rstd_ready, norm.halves + n + 1)
                nc.vector.tensor_tensor(gs[:, b, :], banks[:, 2 * b, :], rstd[:, cols],
                                        ALU.mult).then_inc(gate_scaled, 1)
                dve.wait_ge(up_done, STEPS * c + i + 1)
                nc.vector.tensor_tensor(us[:, b, :], banks[:, 2 * b + 1, :], rstd[:, cols],
                                        ALU.mult).then_inc(up_scaled, 1)
                dve.wait_ge(up_scaled, STEPS * c + i + 1)
                dve.wait_ge(silu_ready, STEPS * c + i + 1)
                nc.vector.tensor_tensor(us[:, b, :], gs[:, b, :], us[:, b, :], ALU.mult).then_inc(prod_ready, 1)
                dve.wait_ge(hid_hi_ready, STEPS * c + i + 1)
                nc.vector.tensor_tensor(hid_lo[:, t, cols], us[:, b, :], hid_hi[:, t, cols].bitcast(F32),
                                        ALU.subtract).then_inc(hid_ready, 1)
            for j in range(OUTS):
                m, cols = halves(j)
                dve.wait_ge(down_done, OUTS * c + j + 1)
                if j == 0 and not first:
                    dve.wait_ge(x_updated, OUTS * c)
                nc.vector.scalar_tensor_tensor(out=xT[:, m, cols], in0=banks[:, 4 + j % 4, :], scalar=0.5,
                                               in1=xT[:, m, cols], op0=ALU.mult,
                                               op1=ALU.add).then_inc(x_updated, 1)
                if not last and j in (2, 5, 8, 11):
                    w_split_dve(dve, f, c + 1, j // 3)

        STEPS_A = 22
        TURNS_AT = {0: (0,), 1: (1,), 6: (2, 3), 7: (4, 5), 9: (6, 7), 10: (8, 9), 11: (10, 11), 12: (12, 13),
                    14: (14, 15), 15: (16, 17), 17: (18, 19), 18: (20, 21), 19: (22, 23), 20: (24, 25)}
        GROUPS = [(h, g, j) for h in range(2) for g in range(2) for j in range(4 * (g + 1))]
        TURNS = 2 + len(GROUPS)
        FIRST_PIECE = 2
        PIECES = ((0, 3), (3, 6), (6, 8))
        SLOT1_AT = {0: 0, 1: 1, 2: 2, 3: 3}
        SLOT0_AT = {9: 0, 10: 1, 12: 2, 14: 3}
        W_AT = {0: 0, 3: 1, 9: 2}
        O_AT = {8: 0, 13: 1, 16: 2, 21: 3}
        TAIL_AT = {1: 0, 2: 1, 3: 2, 4: 3, 5: 4, 6: 5, 7: 6, 9: 7, 11: 8, 13: 9}
        TAIL = KT - 1 + KT

        def pair_load(sp, p, u):
            src = fox_w_in[0, :, bass.ds(u * D + p * P, P)].rearrange("(k p) n -> p k n", p=P)
            sp.dma_start(raw[:, u, :].rearrange("p (k n) -> p k n", n=P), src).then_inc(pw_loaded[u], 16)

        def pw_split_act(act, p, u):
            act.wait_ge(pw_loaded[u], 16 * (p + 1))
            nc.scalar.activation(wa_hi[:, u, :], raw[:, u, :], ACT.Copy).then_inc(pw_hi_ready[u], 1)

        def pw_split_dve(dve, p, u):
            dve.wait_ge(pw_hi_ready[u], p + 1)
            nc.vector.tensor_tensor(wa_lo[:, u, :], raw[:, u, :], wa_hi[:, u, :].bitcast(F32),
                                    ALU.subtract).then_inc(pw_ready[u], 1)

        def project_pe(pe, p, idx, part, bank):
            u, n = divmod(idx, NS)
            if part == 0 and n == 0:
                pe.wait_ge(pw_ready[u], p + 1)
            for k in range(*PIECES[part]):
                w = slice(k * P, (k + 1) * P)
                cols = slice(n * BANK, (n + 1) * BANK)
                mm = three(banks[:, bank, :], wa_hi[:, u, w], wa_lo[:, u, w], hn_hi[:, k, cols], hn_lo[:, k, cols],
                           k == 0, k == KT - 1)
            if part == 2:
                mm.then_inc(proj_done, 1)

        def t_dve(dve, p, idx, bank):
            u, n = divmod(idx, NS)
            cols = slice(n * BANK, (n + 1) * BANK)
            dve.wait_ge(proj_done, 6 * p + idx + 1)
            nc.vector.scalar_tensor_tensor(out=t[:, u, cols], in0=banks[:, bank, :],
                                           scalar=-float(HD) ** -0.5 if u == 0 else 1.0, in1=rstd[:, cols],
                                           op0=ALU.mult, op1=ALU.mult).then_inc(t_ready, 1)

        def aug_act(act, p, h, idx):
            u, n = divmod(idx, NS)
            cols = slice(n * BANK, (n + 1) * BANK)
            rows = slice(h * HD, (h + 1) * HD)
            act.wait_ge(t_ready, 6 * p + idx + 1)
            parts, ext = (q_parts, q_ext) if u == 0 else (k_parts, k_ext)
            own = slice(HD, P) if u == 0 else slice(0, HD)
            nc.scalar.activation(ext[0:HD, h, cols], t[rows, u, cols], ACT.Copy).then_inc(aug_hi_ready[h], 1)
            nc.scalar.activation(parts[own, h, cols], t[rows, u, cols], ACT.Copy).then_inc(aug_hi_ready[h], 1)

        def aug_dve(dve, p, h, idx):
            u, n = divmod(idx, NS)
            cols = slice(n * BANK, (n + 1) * BANK)
            rows = slice(h * HD, (h + 1) * HD)
            dve.wait_ge(aug_hi_ready[h], 8 * p + 2 * idx + 2)
            if u == 0:
                hi, lo = (q_ext[0:HD, h, cols], q_parts[0:HD, h, cols]) if h == 0 else \
                         (q_parts[HD:P, h, cols], q_parts[0:HD, h, cols])
            elif h == 0:
                hi, lo = k_ext[0:HD, h, cols], k_parts[HD:P, h, cols]
            else:
                hi, lo = None, k_parts[HD:P, h, cols]
            if hi is None:
                nc.vector.tensor_copy(o_half[0:HD, :], t[rows, u, cols]).then_inc(moved, 1)
                dve.wait_ge(moved, NS * p + n + 1)
                nc.vector.tensor_tensor(lo, o_half[0:HD, :], k_ext[0:HD, h, cols].bitcast(F32),
                                        ALU.subtract).then_inc(aug_ready[h], 1)
            else:
                nc.vector.tensor_tensor(lo, t[rows, u, cols], hi.bitcast(F32), ALU.subtract).then_inc(aug_ready[h], 1)

        def probs(h, b):
            return p_low[:, b, 0:(b + 1) * P] if b < 4 else p_high[:, b - 4, 0:(b + 1) * P]

        def scores(s):
            b = s % 8
            return banks[:, 2 * (s % 2):2 * (s % 2) + 2, :].rearrange("p a n -> p (a n)")[:, 0:(b + 1) * P]

        def first_col(g, j):
            return max(0, j - 4 * g) * P

        def attend_pe(pe, p, proj):
            for s in range(STEPS_A):
                if s < 16:
                    h, b = divmod(s, 8)
                    if b == 0:
                        pe.wait_ge(aug_ready[h], 4 * (p + 1))
                        pe.wait_ge(ext_loaded[h], 32 * (p + 1))
                    if s >= 2:
                        pe.wait_ge(exp_ready, 16 * p + s - 1)
                    width = (b + 1) * P
                    qs = slice(b * P, (b + 1) * P)
                    for c0 in range(0, width, BANK):
                        c1 = min(width, c0 + BANK)
                        psum = banks[:, 2 * (s % 2) + c0 // BANK, 0:c1 - c0]
                        diagonal = c1 == width
                        nc.tensor.matmul(psum, q_parts[:, h, qs], k_parts[:, h, c0:c1], start=True, stop=False)
                        mm = nc.tensor.matmul(psum, q_ext[0:HD + 4, h, qs], k_ext[0:HD + 4, h, c0:c1],
                                              start=False, stop=not diagonal)
                        if diagonal:
                            mm = nc.tensor.matmul(banks[:, 2 * (s % 2) + c0 // BANK, c1 - c0 - P:c1 - c0],
                                                  ident_r[:], mask[:], start=False, stop=True)
                    mm.then_inc(scores_done, 1)
                for r in TURNS_AT.get(s - 1, ()):
                    if r < 2:
                        continue
                    h, g, j = GROUPS[r - 2]
                    pe.wait_ge(part_ready, TURNS * p + r + 1)
                    if j == 0:
                        pe.wait_ge(o_ready, 4 * p + 2 * h + g + 1)
                    c0 = first_col(g, j)
                    last = j == 4 * g + 3
                    nc.tensor.matmul(banks[:, 6, c0:BANK], v_parts[:, j, h, :, :], pt_hi[:, r % 2, c0:BANK],
                                     start=j == 0, stop=False)
                    nc.tensor.matmul(banks[:, 6, c0:BANK], v_parts[:, j, h, :, :], pt_lo[:, r % 2, c0:BANK],
                                     start=False, stop=last).then_inc(pv_done, 1)
                for r in TURNS_AT.get(s, ()):
                    if r >= 2:
                        pe.wait_ge(part_ready, TURNS * p + r - 1)
                        h, g, j = GROUPS[r - 2]
                        if j == 0:
                            pe.wait_ge(p_ready, 16 * p + 8 * h + 4 * g + 4)
                        for i in range(first_col(g, j) // P, 4):
                            src = (p_high if g else p_low)[:, i, j * P:(j + 1) * P]
                            mm = nc.tensor.transpose(banks[:, 4 + r % 2, i * P:(i + 1) * P], src, ident[:])
                    else:
                        pe.wait_ge(t_ready, 6 * p + 5 + r)
                        for i in range(4):
                            mm = nc.tensor.transpose(banks[:, 4 + r, i * P:(i + 1) * P],
                                                     t[:, 2, r * BANK + i * P:r * BANK + (i + 1) * P], ident[:])
                    mm.then_inc(turned, 1)
                piece = s - FIRST_PIECE
                if proj and 0 <= piece < 18:
                    if piece % 3 == 0:
                        pe.wait_ge(t_ready, 6 * (p + 1) + piece // 3)
                    project_pe(pe, p + 1, piece // 3, piece % 3, 7)

        def attend_act(act, p, proj):
            for s in range(STEPS_A):
                if proj and s in W_AT:
                    pw_split_act(act, p + 1, W_AT[s])
                if s < 16:
                    if s == 12:
                        act.wait_ge(turned, TURNS * p + 14)
                    act.wait_ge(low_ready, 16 * p + s + 1)
                    nc.scalar.activation(probs(s // 8, s % 8), scores(s), ACT.Exp, bias=low[:, s:s + 1], scale=-1.0,
                                         accum_out=rsum[:, s:s + 1]).then_inc(exp_ready, 1)
                for r in TURNS_AT.get(s, ()):
                    act.wait_ge(turned, TURNS * p + r + 1)
                    if r < 2:
                        nc.scalar.activation(v_parts[:, 4 * r:4 * r + 4, :, 0, :],
                                             banks[:, 4 + r, :].rearrange("p (j h d) -> p j h d", j=4, h=2),
                                             ACT.Copy).then_inc(part_hi_ready, 1)
                    else:
                        c0 = first_col(*GROUPS[r - 2][1:])
                        nc.scalar.activation(pt_hi[:, r % 2, c0:BANK], banks[:, 4 + r % 2, c0:BANK],
                                             ACT.Copy).then_inc(part_hi_ready, 1)
                if s in O_AT:
                    act.wait_ge(pv_done, 24 * p + (4, 12, 16, 24)[O_AT[s]])
                    act.wait_ge(o_ready, 4 * p + O_AT[s] + 1)
                    nc.scalar.activation(o_half[0:HD, :], banks[HD:P, 6, :], ACT.Copy).then_inc(o_half_ready, 1)
                if s in SLOT1_AT:
                    aug_act(act, p, 1, SLOT1_AT[s])
                if proj and s in SLOT0_AT:
                    aug_act(act, p + 1, 0, SLOT0_AT[s])
                if not proj and s in TAIL_AT:
                    tail_act(act, TAIL_AT[s])

        def attend_dve(dve, p, proj):
            for s in range(STEPS_A):
                if proj and s in W_AT:
                    pw_split_dve(dve, p + 1, W_AT[s])
                if s < 16:
                    dve.wait_ge(scores_done, 16 * p + s + 1)
                    nc.vector.tensor_reduce(low[:, s:s + 1], scores(s), AX_X, ALU.min).then_inc(low_ready, 1)
                if 1 <= s <= 16:
                    dve.wait_ge(exp_ready, 16 * p + s)
                    nc.vector.reciprocal(rinv[:, s - 1:s], rsum[:, s - 1:s]).then_inc(rinv_ready, 1)
                    dve.wait_ge(rinv_ready, 16 * p + s)
                    pr = probs((s - 1) // 8, (s - 1) % 8)
                    nc.vector.tensor_scalar(pr, pr, rinv[:, s - 1:s], None, ALU.mult).then_inc(p_ready, 1)
                for r in TURNS_AT.get(s, ()):
                    dve.wait_ge(part_hi_ready, TURNS * p + r + 1)
                    if r < 2:
                        blocks = slice(4 * r, 4 * r + 4)
                        for h in range(2):
                            v = nc.vector.tensor_tensor(
                                v_parts[:, blocks, h, 1, :],
                                banks[:, 4 + r, :].rearrange("p (j h d) -> p j h d", j=4, h=2)[:, :, h, :],
                                v_parts[:, blocks, h, 0, :].bitcast(F32), ALU.subtract)
                        v.then_inc(part_ready, 1)
                    else:
                        c0 = first_col(*GROUPS[r - 2][1:])
                        nc.vector.tensor_tensor(pt_lo[:, r % 2, c0:BANK], banks[:, 4 + r % 2, c0:BANK],
                                                pt_hi[:, r % 2, c0:BANK].bitcast(F32),
                                                ALU.subtract).then_inc(part_ready, 1)
                piece = s - FIRST_PIECE
                if proj and 0 <= piece < 18 and piece % 3 == 2:
                    t_dve(dve, p + 1, piece // 3, 7)
                if s in O_AT:
                    h, g = divmod(O_AT[s], 2)
                    if O_AT[s] == 0:
                        dve.wait_ge(oT_free, 16 * (p + 1))
                    dve.wait_ge(o_half_ready, 4 * p + O_AT[s] + 1)
                    nc.vector.tensor_tensor(oT[h * HD:(h + 1) * HD, g * BANK:(g + 1) * BANK], banks[0:HD, 6, :],
                                            o_half[0:HD, :], ALU.add).then_inc(o_ready, 1)
                if s in SLOT1_AT:
                    aug_dve(dve, p, 1, SLOT1_AT[s])
                if proj and s in SLOT0_AT:
                    aug_dve(dve, p + 1, 0, SLOT0_AT[s])
                if not proj and s in TAIL_AT:
                    tail_dve(dve, TAIL_AT[s])

        def pair_pool(pool, p, proj):
            if proj:
                for h in range(2):
                    pool.wait_ge(scores_done, 16 * p + 8 * (h + 1))
                    ext_load(pool, p + 1, h)
            pool.wait_ge(o_ready, 4 * (p + 1) + 1)
            if proj:
                pool.dma_start(o_dram[bass.ds(p, 1), :, :].rearrange("a p s -> (a p) s"), oT[:]).then_inc(oT_free, 16)

        def ext_load(pool, p, h):
            for dst, a in ((k_ext[HD:HD + 2, h, :], 0), (q_ext[HD + 2:HD + 4, h, :], 2)):
                pool.dma_start(dst, ext_dram[bass.ds(2 * p + h, 1), a:a + 2, :].rearrange("h a s -> (h a) s")
                               ).then_inc(ext_loaded[h], 16)

        def tail_place(e):
            if e < KT - 1:
                return hn_hi[:, e, :], hn_lo[:, e, :]
            return wo_unit(e - (KT - 1))

        def wo_unit(m):
            return (wa_hi[:, m, :], wa_lo[:, m, :]) if m < 3 else (wo_hi[:, m - 3, :], wo_lo[:, m - 3, :])

        def tail_sync(sp):
            for e in range(TAIL):
                if e < RAW:
                    sp.wait_ge(pw_ready[e], PAIRS)
                else:
                    sp.wait_ge(tail_ready, e - RAW + 1)
                slot = raw[:, e % RAW, :]
                if e < KT - 1:
                    sp.wait_ge(oT_free, 16 * (e + 2))
                    sp.dma_start(slot, o_dram[e]).then_inc(tail_loaded[e % RAW], 16)
                else:
                    m = e - (KT - 1)
                    sp.dma_start(slot.rearrange("p (k n) -> p k n", n=P),
                                 fox_w_o[0, :, m * P:(m + 1) * P].rearrange("(k p) n -> p k n", p=P)
                                 ).then_inc(tail_loaded[e % RAW], 16)

        def tail_act(act, e):
            act.wait_ge(tail_loaded[e % RAW], 16 * (e // RAW + 1))
            nc.scalar.activation(tail_place(e)[0], raw[:, e % RAW, :], ACT.Copy).then_inc(tail_hi_ready, 1)

        def tail_dve(dve, e):
            dve.wait_ge(tail_hi_ready, e + 1)
            hi, lo = tail_place(e)
            nc.vector.tensor_tensor(lo, raw[:, e % RAW, :], hi.bitcast(F32), ALU.subtract).then_inc(tail_ready, 1)

        def wo_pe(pe):
            for j in range(OUTS):
                n, m = divmod(j, KT)
                cols = slice(n * BANK, (n + 1) * BANK)
                if n == 0:
                    pe.wait_ge(tail_ready, KT + m)
                if j >= 4:
                    pe.wait_ge(wo_added, j - 3)
                hi, lo = wo_unit(m)
                for k in range(KT):
                    if j == 0 and k == KT - 1:
                        pe.wait_ge(o7_ready, 1)
                    w = slice(k * P, (k + 1) * P)
                    mm = three(banks[:, 4 + j % 4, :], hi[:, w], lo[:, w], hn_hi[:, k, cols], hn_lo[:, k, cols],
                               k == 0, k == KT - 1)
                mm.then_inc(wo_done, 1)

        block = ctx.enter_context(nc.Block())

        @block.sync
        def _(sp):
            for b in range(SB):
                if b >= 4:
                    sp.wait_ge(x_turned, 2 * (b - 3))
                sp.dma_start(xin[:, b % 4, :], x[0, b * P:(b + 1) * P, :]).then_inc(x_loaded[b % 4], 16)
                if b == 3:
                    for u in range(RAW):
                        ffn_load(sp, ffn1, 0, u)
            ffn_sync(sp, ffn1)
            for u in range(RAW):
                sp.wait_ge(w_ready[u + RAW], CHUNKS)
                pair_load(sp, 0, u)
            for kt in range(KT):
                sp.wait_ge(x_updated, OUTS * (CHUNKS - 1) + KT + kt + 1)
                sp.dma_start(x_dram[kt], xT[:, kt, :]).then_inc(x_spilled, 16)
            with sp.Fori(0, PAIRS - 1) as p:
                for u in range(3):
                    sp.wait_ge(pw_ready[u], p + 1)
                    pair_load(sp, p + 1, u)
            tail_sync(sp)
            for u in range(RAW):
                sp.wait_ge(tail_ready, TAIL - RAW + u + 1)
                ffn_load(sp, ffn2, CHUNKS, u)
            ffn_sync(sp, ffn2)
            for b in range(SB):
                sp.wait_ge(yout_act, b + 1)
                sp.wait_ge(yout_dve, b + 1)
                sp.dma_start(out[0, b * P:(b + 1) * P, :], yout[:, b % 2, :]).then_inc(stored[b % 2], 16)
            for i in range(2):
                sp.wait_ge(stored[i], 16 * SB // 2)

        @block.gpsimd
        def _(pool):
            for i, g in enumerate((norm_ffn1[0, :], norm_mix[0, :], norm_ffn2[0, :], norm_final)):
                pool.dma_start(gain_rows[i * KT:(i + 1) * KT, :],
                               g.rearrange("(k p) -> k p", p=P)).then_inc(gains_loaded, 16)
            nc.gpsimd.memset(ident[:], 0.0).then_inc(ident_made, 1)
            pool.wait_ge(ident_made, 1)
            nc.gpsimd.affine_select(out=ident[:], in_=ident[:], compare_op=ALU.not_equal, fill=1.0, base=0,
                                    pattern=[[-1, P]], channel_multiplier=1).then_inc(ident_made, 1)
            pool.dma_start(b_f[:], fox_b_f.rearrange("a h -> h a")).then_inc(gate_in_loaded, 16)
            pool.dma_start(wf_raw[:], fox_w_in[0, :, 3 * D:3 * D + NH].rearrange("(k p) n -> p k n", p=P)
                           ).then_inc(gate_in_loaded, 16)
            nc.gpsimd.memset(mask0[:], 0.0).then_inc(mask_made, 1)
            pool.wait_ge(mask_made, 1)
            nc.gpsimd.affine_select(out=mask0[:], in_=mask0[:], compare_op=ALU.is_ge, fill=1e38, base=0,
                                    pattern=[[-1, P]], channel_multiplier=1).then_inc(mask_made, 1)
            norm_pool(pool, norm1)
            norm_pool(pool, norm2)
            pool.wait_ge(f_step, 8)
            pool.dma_start(ext_dram, ext_rows[:]).then_inc(oT_free, 16)
            pool.wait_ge(oT_free, 16)
            pool.wait_ge(rows_one, 2)
            for h in range(2):
                ext_load(pool, 0, h)
            with pool.Fori(0, PAIRS - 1) as p:
                pair_pool(pool, p, True)
            pool.wait_ge(scores_done, 16 * PAIRS)
            for kt in range(KT):
                pool.dma_start(xT[:, kt, :], x_dram[kt]).then_inc(x_back[kt], 16)
            norm_pool(pool, norm3)
            norm_pool(pool, normf)

        @block.tensor
        def _(pe):
            pe.wait_ge(ident_made, 2)
            pe.wait_ge(gains_loaded, 64)
            nc.tensor.transpose(banks[:, 7, 0:4 * KT], gain_rows[:], ident[0:4 * KT, 0:4 * KT]).then_inc(gains_turned, 1)
            for b in range(SB):
                pe.wait_ge(x_loaded[b % 4], 16 * (b // 4 + 1))
                for h in range(2):
                    if b >= 2:
                        pe.wait_ge(x_kept_dve if h else x_kept_act, b - 1)
                    for i in range(4):
                        mm = nc.tensor.transpose(banks[:, 2 * (b % 2) + h, i * P:(i + 1) * P],
                                                 xin[:, b % 4, (4 * h + i) * P:(4 * h + i + 1) * P], ident[:])
                    mm.then_inc(x_turned, 1)
            pe.wait_ge(x_kept_act, SB)
            pe.wait_ge(x_kept_dve, SB)
            pe.wait_ge(ones_made, 1)
            ffn_pe(pe, ffn1, norm1, 0, first=True)
            with pe.Fori(1, CHUNKS) as c:
                ffn_pe(pe, ffn1, norm1, c)
            for n in range(NS):
                cols = slice(n * BANK, (n + 1) * BANK)
                if n == 0:
                    pe.wait_ge(wf_ready, 1)
                for k in range(KT):
                    pe.wait_ge(hn_ready, norm2.tiles + n * KT + k + 1)
                    mm = three(banks[0:NH, 6 + n, :], wf_hi[:, k, :], wf_lo[:, k, :], hn_hi[:, k, cols],
                               hn_lo[:, k, cols], k == 0, k == KT - 1)
                mm.then_inc(f_done, 1)
                stat_pe(pe, norm2, n)
            for idx in range(6):
                if idx == 4:
                    pe.wait_ge(var_ready, norm2.halves + 2)
                for part in range(3):
                    project_pe(pe, 0, idx, part, idx)
            pe.wait_ge(ident_r_made, 2)
            with pe.Fori(0, PAIRS - 1) as p:
                attend_pe(pe, p, True)
            attend_pe(pe, PAIRS - 1, False)
            wo_pe(pe)
            ffn_pe(pe, ffn2, norm3, CHUNKS, first=True)
            with pe.Fori(CHUNKS + 1, 2 * CHUNKS) as c:
                ffn_pe(pe, ffn2, norm3, c)
            for n in range(NS):
                stat_pe(pe, normf, n)
            for b in range(SB):
                n, i = divmod(b, 4)
                if i == 0:
                    pe.wait_ge(y_ready, KT * (n + 1))
                for h in range(2):
                    if b >= 2:
                        pe.wait_ge(yout_dve if h else yout_act, b - 1)
                    for k in range(4):
                        mm = nc.tensor.transpose(banks[:, 2 * (b % 2) + h, k * P:(k + 1) * P],
                                                 y[:, 4 * h + k, i * P:(i + 1) * P], ident[:])
                    mm.then_inc(y_turned, 1)

        @block.scalar
        def _(act):
            for b in range(SB):
                act.wait_ge(x_turned, 2 * b + 1)
                nc.scalar.activation(xT[:, 0:4, b * P:(b + 1) * P],
                                     banks[:, 2 * (b % 2), :].rearrange("p (k s) -> p k s", k=4),
                                     ACT.Copy).then_inc(x_kept_act, 1)
            act.wait_ge(gains_ready, 1)
            act.wait_ge(x_kept_act, SB)
            act.wait_ge(x_kept_dve, SB)
            for j in range(NS * KT):
                norm_act(norm1, j)
                square_act(act, norm1, j)
                if j in (1, 3, 5, 7):
                    w_split_act(act, ffn1, 0, j // 2)
                if j % KT == KT - 1:
                    stat_split_act(act, norm1, j // KT)
            ffn_act(act, ffn1, norm1, 0, first=True)
            with act.Fori(1, CHUNKS - 1) as c:
                ffn_act(act, ffn1, norm1, c)
            ffn_act(act, ffn1, norm1, CHUNKS - 1, last=True)
            act.wait_ge(gate_in_loaded, 32)
            nc.scalar.activation(wf_hi[:], wf_raw[:], ACT.Copy).then_inc(wf_hi_ready, 1)
            act.wait_ge(up_done, STEPS * CHUNKS)
            pw_split_act(act, 0, 0)
            for j in range(NS * KT):
                act.wait_ge(x_updated, OUTS * (CHUNKS - 1) + j + 1)
                norm_act(norm2, j)
                square_act(act, norm2, j)
                if j % KT == KT - 1:
                    stat_split_act(act, norm2, j // KT)
            for n in range(NS):
                rstd_act(act, norm2, n)
            for u in (1, 2):
                pw_split_act(act, 0, u)
            act.wait_ge(f_step, 3)
            nc.scalar.activation(ez[:], z[:], ACT.Abs).then_inc(f_act, 1)
            act.wait_ge(f_act, 1)
            nc.scalar.activation(ez[:], ez[:], ACT.Exp, scale=-1.0).then_inc(f_act, 1)
            act.wait_ge(f_act, 2)
            nc.scalar.activation(ez[:], ez[:], ACT.Ln, bias=1.0).then_inc(f_act, 1)
            act.wait_ge(f_step, 5)
            nc.scalar.activation(ext_rows[:, 0, :], cum[:], ACT.Copy).then_inc(f_act, 1)
            nc.scalar.activation(ext_rows[:, 2, :], cum[:], ACT.Copy, scale=-1.0).then_inc(f_act, 1)
            act.wait_ge(x_spilled, 16 * KT)
            for idx in range(4):
                aug_act(act, 0, 0, idx)
            with act.Fori(0, PAIRS - 1) as p:
                attend_act(act, p, True)
            attend_act(act, PAIRS - 1, False)
            act.wait_ge(o_ready, 4 * PAIRS + 1)
            nc.scalar.activation(hn_hi[:, KT - 1, :], oT[:], ACT.Copy).then_inc(o7_hi_ready, 1)
            for e in range(len(TAIL_AT), TAIL):
                tail_act(act, e)
            for j in range(NS * KT):
                if j % KT == 0:
                    act.wait_ge(wo_done, KT * (j // KT + 1))
                    if j:
                        w_split_act(act, ffn2, CHUNKS, 3)
                act.wait_ge(wo_added, j + 1)
                norm_act(norm3, j)
                square_act(act, norm3, j)
                if j % KT == KT - 1:
                    stat_split_act(act, norm3, j // KT)
                if j == KT - 1:
                    act.wait_ge(wo_done, KT + 3)
                    for u in range(3):
                        w_split_act(act, ffn2, CHUNKS, u)
            ffn_act(act, ffn2, norm3, CHUNKS, first=True)
            with act.Fori(CHUNKS + 1, 2 * CHUNKS - 1) as c:
                ffn_act(act, ffn2, norm3, c)
            ffn_act(act, ffn2, norm3, 2 * CHUNKS - 1, last=True)
            for j in range(NS * KT):
                act.wait_ge(x_updated, OUTS * (2 * CHUNKS - 1) + j + 1)
                square_act(act, normf, j)
                if j % KT == KT - 1:
                    stat_split_act(act, normf, j // KT)
            for n in range(NS):
                rstd_act(act, normf, n)
            for b in range(SB):
                act.wait_ge(y_turned, 2 * b + 1)
                if b >= 2:
                    act.wait_ge(stored[b % 2], 16 * (b // 2))
                nc.scalar.activation(yout[:, b % 2, 0:BANK], banks[:, 2 * (b % 2), :],
                                     ACT.Copy).then_inc(yout_act, 1)

        @block.vector
        def _(dve):
            nc.vector.memset(ones[:].bitcast(F32), 1.0).then_inc(ones_made, 1)
            dve.wait_ge(ident_made, 2)
            nc.vector.tensor_copy(ident_r[:], ident[:]).then_inc(ident_r_made, 1)
            dve.wait_ge(mask_made, 2)
            nc.vector.tensor_copy(mask[:], mask0[:]).then_inc(ident_r_made, 1)
            dve.wait_ge(gains_turned, 1)
            nc.vector.tensor_copy(gains[:], banks[:, 7, 0:4 * KT]).then_inc(gains_ready, 1)
            dve.wait_ge(gains_ready, 1)
            for b in range(SB):
                dve.wait_ge(x_turned, 2 * b + 2)
                nc.vector.tensor_copy(xT[:, 4:8, b * P:(b + 1) * P],
                                      banks[:, 2 * (b % 2) + 1, :].rearrange("p (k s) -> p k s", k=4)
                                      ).then_inc(x_kept_dve, 1)
            for j in range(NS * KT):
                norm_dve(dve, norm1, j)
                if j in (1, 3, 5, 7):
                    w_split_dve(dve, ffn1, 0, j // 2)
            for n in range(NS):
                stat_split_dve(dve, norm1, n)
            ffn_dve(dve, ffn1, norm1, 0, first=True)
            with dve.Fori(1, CHUNKS - 1) as c:
                ffn_dve(dve, ffn1, norm1, c)
            ffn_dve(dve, ffn1, norm1, CHUNKS - 1, last=True)
            dve.wait_ge(wf_hi_ready, 1)
            nc.vector.tensor_tensor(wf_lo[:], wf_raw[:], wf_hi[:].bitcast(F32), ALU.subtract).then_inc(wf_ready, 1)
            pw_split_dve(dve, 0, 0)
            for n in range(NS):
                for j in range(n * KT, (n + 1) * KT):
                    norm_dve(dve, norm2, j)
                stat_split_dve(dve, norm2, n)
            for n in range(NS):
                rstd_dve(dve, norm2, n)
            for u in (1, 2):
                pw_split_dve(dve, 0, u)
            for n in range(NS):
                cols = slice(n * BANK, (n + 1) * BANK)
                dve.wait_ge(f_done, n + 1)
                dve.wait_ge(rstd_ready, norm2.halves + n + 1)
                nc.vector.tensor_tensor(z[:, cols], banks[0:NH, 6 + n, :], rstd[0:NH, cols],
                                        ALU.mult).then_inc(f_step, 1)
            dve.wait_ge(f_step, 2)
            nc.vector.tensor_scalar(z[:], z[:], b_f[:], None, ALU.add).then_inc(f_step, 1)
            dve.wait_ge(f_act, 3)
            nc.vector.scalar_tensor_tensor(out=z[:], in0=z[:], scalar=0.0, in1=ez[:], op0=ALU.min,
                                           op1=ALU.subtract).then_inc(f_step, 1)
            dve.wait_ge(f_step, 4)
            nc.vector.tensor_tensor_scan(cum[:], ones[0:NH, 0:1].bitcast(F32).to_broadcast([NH, S]), z[:], 0.0,
                                         ALU.mult, ALU.add).then_inc(f_step, 1)
            dve.wait_ge(f_step, 5)
            dve.wait_ge(f_act, 5)
            nc.vector.tensor_tensor(ext_rows[:, 1, :], cum[:], ext_rows[:, 0, :].bitcast(F32),
                                    ALU.subtract).then_inc(f_step, 1)
            dve.wait_ge(f_step, 6)
            nc.vector.tensor_scalar(ext_rows[:, 3, :], ext_rows[:, 1, :].bitcast(F32), -1.0, None,
                                    ALU.mult).then_inc(f_step, 2)
            for idx in range(6):
                t_dve(dve, 0, idx, idx)
            dve.wait_ge(x_spilled, 16 * KT)
            nc.vector.memset(k_ext[HD:HD + 4, :, :].bitcast(F32), 1.0).then_inc(rows_one, 1)
            nc.vector.memset(q_ext[HD:HD + 4, :, :].bitcast(F32), 1.0).then_inc(rows_one, 1)
            for idx in range(4):
                aug_dve(dve, 0, 0, idx)
            nc.vector.tensor_copy(rinv[:], rstd[:, 0:16]).then_inc(o_ready, 1)
            with dve.Fori(0, PAIRS - 1) as p:
                attend_dve(dve, p, True)
            attend_dve(dve, PAIRS - 1, False)
            dve.wait_ge(o7_hi_ready, 1)
            nc.vector.tensor_tensor(hn_lo[:, KT - 1, :], oT[:], hn_hi[:, KT - 1, :].bitcast(F32),
                                    ALU.subtract).then_inc(o7_ready, 1)
            for e in range(len(TAIL_AT), TAIL):
                tail_dve(dve, e)
            for j in range(NS * KT):
                m, cols = halves(j)
                dve.wait_ge(wo_done, j + 1)
                if j < KT:
                    dve.wait_ge(x_back[j], 16)
                nc.vector.tensor_tensor(xT[:, m, cols], banks[:, 4 + j % 4, :], xT[:, m, cols],
                                        ALU.add).then_inc(wo_added, 1)
                if j >= KT:
                    norm_dve(dve, norm3, j - KT)
            stat_split_dve(dve, norm3, 0)
            for u in range(4):
                w_split_dve(dve, ffn2, CHUNKS, u)
            for j in range(KT, NS * KT):
                norm_dve(dve, norm3, j)
            stat_split_dve(dve, norm3, 1)
            ffn_dve(dve, ffn2, norm3, CHUNKS, first=True)
            with dve.Fori(CHUNKS + 1, 2 * CHUNKS - 1) as c:
                ffn_dve(dve, ffn2, norm3, c)
            ffn_dve(dve, ffn2, norm3, 2 * CHUNKS - 1, last=True)
            for n in range(NS):
                stat_split_dve(dve, normf, n)
            for n in range(NS):
                rstd_dve(dve, normf, n)
            for n in range(NS):
                cols = slice(n * BANK, (n + 1) * BANK)
                dve.wait_ge(rstd_ready, normf.halves + n + 1)
                if n:
                    dve.wait_ge(y_turned, 8 * n)
                for k in range(KT):
                    nc.vector.scalar_tensor_tensor(
                        out=y[:, k, :], in0=xT[:, k, cols], scalar=gains[:, normf.gain + k:normf.gain + k + 1],
                        in1=rstd[:, cols], op0=ALU.mult, op1=ALU.mult).then_inc(y_ready, 1)
                for b in range(4 * n, 4 * n + 4):
                    dve.wait_ge(y_turned, 2 * b + 2)
                    if b >= 2:
                        dve.wait_ge(stored[b % 2], 16 * (b // 2))
                    nc.vector.tensor_copy(yout[:, b % 2, BANK:D], banks[:, 2 * (b % 2) + 1, :]).then_inc(yout_dve, 1)


_INS = ["x", "norm_ffn1", "norm_mix", "norm_ffn2", "norm_final",
        "ffn1_w_gate", "ffn1_w_up", "ffn1_w_down", "ffn2_w_gate", "ffn2_w_up", "ffn2_w_down",
        "fox_w_in", "fox_b_f", "fox_w_o"]


def kernel(**inputs):
    import numpy as _np
    import concourse.bacc as _bacc
    from concourse import mybir as _mybir
    from concourse.bass_utils import run_bass_kernel_spmd as _run

    nc = _bacc.Bacc("TRN2", target_bir_lowering=False, num_devices=1)
    arrays, args = {}, []
    for name in _INS:
        a = _np.ascontiguousarray(inputs[name])
        arrays[f"in_{name}_dram"] = a
        args.append(nc.dram_tensor(f"in_{name}_dram", a.shape, _mybir.dt.from_np(a.dtype), kind="ExternalInput").ap())
    shape = arrays["in_x_dram"].shape
    args.append(nc.dram_tensor("out_dram", shape, _mybir.dt.float32, kind="ExternalOutput").ap())
    build(nc, *args)
    r = _run(nc, [arrays], core_ids=[0])
    return r.results[0]["out_dram"]
```

```python
from contextlib import ExitStack

import concourse.bass as bass
from concourse import mybir

ALU = mybir.AluOpType
ACT = mybir.ActivationFunctionType
AX_X = mybir.AxisListType.X
F32 = mybir.dt.float32
F32R = mybir.dt.float32r

P = 128
BANK = 512
KIB = 1024
EPS = 1e-6


def build(nc, x, norm_ffn1, norm_mix, norm_ffn2, norm_final,
          ffn1_w_gate, ffn1_w_up, ffn1_w_down, ffn2_w_gate, ffn2_w_up, ffn2_w_down,
          fox_w_in, fox_b_f, fox_w_o, out):
    _, S, D = x.shape
    F = ffn1_w_gate.shape[2]
    KT = D // P
    NS = S // BANK
    SB = S // P
    FC = 2 * P
    CHUNKS = F // FC
    assert F % FC == 0 and KT == 8 and NS == 2 and CHUNKS >= 3
    UNITS = 6
    RAW = 3
    STEPS = 2 * NS
    OUTS = NS * KT
    NH = fox_b_f.shape[1]
    HD = D // NH
    PAIRS = NH // 2
    assert HD == 64 and PAIRS == KT and S == 1024

    ctx = ExitStack()
    with ctx:
        def sem(name):
            return ctx.enter_context(nc.semaphore(name))

        arena = ctx.enter_context(nc.sbuf_tensor("arena", [P, 207 * 256], F32))
        base = 16512 if not hasattr(arena, "offset_bytes") else 16512

        def at(name, shape, dt, kib):
            return nc.alloc_sbuf_tensor_at(name, shape, dt, offset=int(base + kib * KIB))

        hn_hi = at("hn_hi", [P, KT, S], F32R, 0)
        hn_lo = at("hn_lo", [P, KT, S], F32R, 32)
        rstd = at("rstd", [P, S], F32, 64)
        raw = at("raw", [P, RAW, 1024], F32, 68)
        wa_hi = at("wa_hi", [P, 3, 1024], F32R, 80)
        wa_lo = at("wa_lo", [P, 3, 1024], F32R, 92)
        ident = at("ident", [P, P], F32, 104)
        ones = at("ones", [P, P], F32R, 104.5)
        gain_rows = at("gain_rows", [4 * KT, P], F32, 105)
        gains = at("gains", [P, 4 * KT], F32, 105.5)
        xT = at("xT", [P, KT, S], F32, 106)
        wb_hi = at("wb_hi", [P, 3, 1024], F32R, 138)
        wb_lo = at("wb_lo", [P, 3, 1024], F32R, 150)
        hid_hi = at("hid_hi", [P, 2, S], F32R, 162)
        hid_lo = at("hid_lo", [P, 2, S], F32R, 170)
        gs = at("gs", [P, 2, BANK], F32, 178)
        us = at("us", [P, 2, BANK], F32, 182)
        sq = at("sq", [P, 2, BANK], F32, 186)
        ssum = at("ssum", [P, NS, BANK], F32, 190)
        ssum_hi = at("ssum_hi", [P, NS, BANK], F32R, 194)
        ssum_lo = at("ssum_lo", [P, NS, BANK], F32R, 198)
        xin = at("xin", [P, SB, D], F32, 138)
        y = at("y", [P, NS, KT, BANK], F32, 0)
        yout = at("yout", [P, SB, D], F32, 32)
        rstd_col = at("rstd_col", [P, SB], F32, 206.5)

        k_parts = at("k_parts", [P, 2, S], F32R, 106)
        k_ext = at("k_ext", [P, 2, S], F32R, 114)
        q_parts = at("q_parts", [P, 2, S], F32R, 122)
        q_ext = at("q_ext", [P, 2, S], F32R, 130)
        t = at("t", [P, 3, S], F32, 138)
        v_parts = at("v_parts", [P, SB, 2, 2, HD], F32R, 150)
        p_low = at("p_low", [P, 4, BANK], F32, 158)
        p_high = at("p_high", [P, 4, S], F32, 166)
        pt_hi = at("pt_hi", [P, 4, BANK], F32R, 182)
        pt_lo = at("pt_lo", [P, 4, BANK], F32R, 190)
        oT = at("oT", [P, S], F32, 198)
        o_half = at("o_half", [P, BANK], F32, 203)
        wo_hi = at("wo_hi", [P, 5, 1024], F32R, 138)
        wo_lo = at("wo_lo", [P, 5, 1024], F32R, 158)
        z = at("z", [NH, S], F32, 158)
        ez = at("ez", [NH, S], F32, 162)
        cum = at("cum", [NH, S], F32, 166)
        ext_rows = at("ext_rows", [NH, 4, S], F32R, 170)
        ident_r = at("ident_r", [P, P], F32R, 202)
        mask = at("mask", [P, P], F32R, 202.5)
        wf_raw = at("wf_raw", [P, KT, NH], F32, 203)
        wf_hi = at("wf_hi", [P, KT, NH], F32R, 203.5)
        wf_lo = at("wf_lo", [P, KT, NH], F32R, 204)
        b_f = at("b_f", [NH, 1], F32, 205)
        low = at("low", [P, 16], F32, 205.25)
        rsum = at("rsum", [P, 16], F32, 205.5)
        rinv = at("rinv", [P, 16], F32, 205.75)
        mask0 = at("mask0", [P, P], F32, 206)
        ext_dram = nc.dram_tensor("ext_rows_scratch", [NH, 4, S], F32R, kind="Internal").ap()
        x_dram = nc.dram_tensor("x_scratch", [KT, P, S], F32, kind="Internal").ap()
        o_dram = nc.dram_tensor("o_scratch", [KT, P, S], F32, kind="Internal").ap()

        banks = ctx.enter_context(nc.psum_tensor("banks", [P, 8, BANK], F32))

        def whi(u):
            return wa_hi[:, u, :] if u < 3 else wb_hi[:, u - 3, :]

        def wlo(u):
            return wa_lo[:, u, :] if u < 3 else wb_lo[:, u - 3, :]

        gains_loaded = sem("gains_loaded")
        ident_made = sem("ident_made")
        ones_made = sem("ones_made")
        gains_turned = sem("gains_turned")
        gains_ready = sem("gains_ready")
        x_loaded = [sem(f"x_loaded{b}") for b in range(SB)]
        x_turned = sem("x_turned")
        x_kept_act = sem("x_kept_act")
        x_kept_dve = sem("x_kept_dve")

        hn_hi_ready = sem("hn_hi_ready")
        hn_ready = sem("hn_ready")
        sq_ready = sem("sq_ready")
        sq_summed = sem("sq_summed")
        ssum_hi_ready = sem("ssum_hi_ready")
        ssum_ready = sem("ssum_ready")
        stat_ready = sem("stat_ready")
        var_ready = sem("var_ready")
        inv_ready = sem("inv_ready")
        rstd_ready = sem("rstd_ready")
        w_loaded = [sem(f"w_loaded{u}") for u in range(UNITS)]
        w_hi_ready = [sem(f"w_hi_ready{u}") for u in range(UNITS)]
        w_ready = [sem(f"w_ready{u}") for u in range(UNITS)]
        gate_done = sem("gate_done")
        up_done = sem("up_done")
        gate_scaled = sem("gate_scaled")
        up_scaled = sem("up_scaled")
        silu_ready = sem("silu_ready")
        prod_ready = sem("prod_ready")
        hid_hi_ready = sem("hid_hi_ready")
        hid_ready = sem("hid_ready")
        down_done = sem("down_done")
        x_updated = sem("x_updated")

        class Norm:
            def __init__(self, index):
                self.gain = index * KT
                self.tiles = index * NS * KT
                self.halves = index * NS

        class Ffn:
            def __init__(self, start, gate, up, down):
                self.start, self.gate, self.up, self.down = start, gate, up, down

        norm1, norm2, norm3, normf = (Norm(i) for i in range(4))
        ffn1 = Ffn(0, ffn1_w_gate, ffn1_w_up, ffn1_w_down)
        ffn2 = Ffn(CHUNKS, ffn2_w_gate, ffn2_w_up, ffn2_w_down)
        assert KT * NS == OUTS
        gate_in_loaded = sem("gate_in_loaded")
        ident_r_made = sem("ident_r_made")
        mask_made = sem("mask_made")
        wf_hi_ready = sem("wf_hi_ready")
        wf_ready = sem("wf_ready")
        f_done = sem("f_done")
        f_step = sem("f_step")
        f_act = sem("f_act")
        ext_stored = sem("ext_stored")
        x_spilled = sem("x_spilled")
        rows_zero = sem("rows_zero")
        rows_one = sem("rows_one")
        ext_loaded = [sem(f"ext_loaded{h}") for h in range(2)]
        pw_loaded = [sem(f"pw_loaded{u}") for u in range(3)]
        pw_hi_ready = [sem(f"pw_hi_ready{u}") for u in range(3)]
        pw_ready = [sem(f"pw_ready{u}") for u in range(3)]
        proj_done = sem("proj_done")
        t_ready = sem("t_ready")
        aug_hi_ready = [sem(f"aug_hi_ready{h}") for h in range(2)]
        aug_ready = [sem(f"aug_ready{h}") for h in range(2)]
        scores_done = sem("scores_done")
        low_ready = sem("low_ready")
        exp_ready = sem("exp_ready")
        rinv_ready = sem("rinv_ready")
        p_ready = sem("p_ready")
        turned = sem("turned")
        part_hi_ready = sem("part_hi_ready")
        part_ready = sem("part_ready")
        pv_done = sem("pv_done")
        o_half_ready = sem("o_half_ready")
        o_ready = sem("o_ready")
        oT_free = sem("oT_free")
        tail_loaded = [sem(f"tail_loaded{i}") for i in range(RAW)]
        tail_hi_ready = sem("tail_hi_ready")
        tail_ready = sem("tail_ready")
        o7_hi_ready = sem("o7_hi_ready")
        o7_ready = sem("o7_ready")
        x_back = [sem(f"x_back{k}") for k in range(KT)]
        wo_done = sem("wo_done")
        wo_added = sem("wo_added")
        y_ready = sem("y_ready")
        y_turned = sem("y_turned")
        yout_act = sem("yout_act")
        yout_dve = sem("yout_dve")
        stored = sem("stored")

        def halves(j):
            n, kt = divmod(j, KT)
            return kt, slice(n * BANK, (n + 1) * BANK)

        def norm_act(norm, j):
            kt, cols = halves(j)
            nc.scalar.activation(hn_hi[:, kt, cols], xT[:, kt, cols], ACT.Copy,
                                 scale=gains[:, norm.gain + kt:norm.gain + kt + 1]).then_inc(hn_hi_ready, 1)

        def square_act(act, norm, j):
            kt, cols = halves(j)
            if j >= 2:
                act.wait_ge(sq_summed, norm.tiles + j - 1)
            nc.scalar.activation(sq[:, j % 2, :], xT[:, kt, cols], ACT.Square).then_inc(sq_ready, 1)

        def norm_dve(dve, norm, j):
            kt, cols = halves(j)
            dve.wait_ge(hn_hi_ready, norm.tiles + j + 1)
            nc.vector.scalar_tensor_tensor(
                out=hn_lo[:, kt, cols], in0=xT[:, kt, cols], scalar=gains[:, norm.gain + kt:norm.gain + kt + 1],
                in1=hn_hi[:, kt, cols].bitcast(F32), op0=ALU.mult, op1=ALU.subtract).then_inc(hn_ready, 1)

        def norm_pool(pool, norm):
            for j in range(NS * KT):
                n, kt = divmod(j, KT)
                pool.wait_ge(sq_ready, norm.tiles + j + 1)
                if kt == 0:
                    nc.gpsimd.tensor_copy(ssum[:, n, :], sq[:, j % 2, :]).then_inc(sq_summed, 1)
                else:
                    pool.wait_ge(sq_summed, norm.tiles + j)
                    nc.gpsimd.tensor_tensor(ssum[:, n, :], ssum[:, n, :], sq[:, j % 2, :],
                                            ALU.add).then_inc(sq_summed, 1)

        def stat_split_act(act, norm, n):
            act.wait_ge(sq_summed, norm.tiles + KT * (n + 1))
            nc.scalar.activation(ssum_hi[:, n, :], ssum[:, n, :], ACT.Copy).then_inc(ssum_hi_ready, 1)

        def stat_split_dve(dve, norm, n):
            dve.wait_ge(ssum_hi_ready, norm.halves + n + 1)
            nc.vector.tensor_tensor(ssum_lo[:, n, :], ssum[:, n, :], ssum_hi[:, n, :].bitcast(F32),
                                    ALU.subtract).then_inc(ssum_ready, 1)

        def stat_pe(pe, norm, n):
            pe.wait_ge(ssum_ready, norm.halves + n + 1)
            nc.tensor.matmul(banks[:, 4 + n, :], ones[:], ssum_hi[:, n, :], start=True, stop=False)
            nc.tensor.matmul(banks[:, 4 + n, :], ones[:], ssum_lo[:, n, :], start=False,
                             stop=True).then_inc(stat_ready, 1)

        def rstd_dve(dve, norm, n):
            cols = slice(n * BANK, (n + 1) * BANK)
            dve.wait_ge(stat_ready, norm.halves + n + 1)
            nc.vector.tensor_scalar(rstd[:, cols], banks[:, 4 + n, :], 1.0 / D, EPS, ALU.mult,
                                    ALU.add).then_inc(var_ready, 1)
            dve.wait_ge(var_ready, norm.halves + n + 1)
            nc.vector.reciprocal(rstd[:, cols], rstd[:, cols]).then_inc(inv_ready, 1)

        def rstd_act(act, norm, n):
            cols = slice(n * BANK, (n + 1) * BANK)
            act.wait_ge(inv_ready, norm.halves + n + 1)
            nc.scalar.activation(rstd[:, cols], rstd[:, cols], ACT.Sqrt).then_inc(rstd_ready, 1)

        def ffn_load(sp, f, c, u):
            at_chunk = (c - f.start) * FC
            dst = raw[:, u % RAW, :]
            if u < 4:
                w = f.gate if u < 2 else f.up
                half = (u % 2) * (D // 2)
                src = w[0, half:half + D // 2, bass.ds(at_chunk, FC)].rearrange("(k p) n -> p k n", p=P)
                dst = dst.rearrange("p (k n) -> p k n", n=FC)
            else:
                src = f.down[0, bass.ds(at_chunk + (u - 4) * P, P), :]
            sp.dma_start(dst, src).then_inc(w_loaded[u], 16)

        def ffn_sync(sp, f):
            for u in range(RAW, UNITS):
                sp.wait_ge(w_ready[u - RAW], f.start + 1)
                ffn_load(sp, f, f.start, u)
            with sp.Fori(f.start + 1, f.start + CHUNKS) as c:
                for u in range(UNITS):
                    if u >= RAW:
                        sp.wait_ge(w_ready[u - RAW], c + 1)
                    else:
                        sp.wait_ge(w_ready[u + RAW], c)
                    ffn_load(sp, f, c, u)

        def w_split_act(act, f, c, u):
            act.wait_ge(w_loaded[u], 16 * (c + 1))
            nc.scalar.activation(whi(u), raw[:, u % RAW, :], ACT.Copy).then_inc(w_hi_ready[u], 1)

        def w_split_dve(dve, f, c, u):
            dve.wait_ge(w_hi_ready[u], c + 1)
            nc.vector.tensor_tensor(wlo(u), raw[:, u % RAW, :], whi(u).bitcast(F32),
                                    ALU.subtract).then_inc(w_ready[u], 1)

        def three(psum, hi, lo, x_hi, x_lo, first, last):
            nc.tensor.matmul(psum, hi, x_lo, start=first, stop=False)
            nc.tensor.matmul(psum, hi, x_hi, start=False, stop=False)
            return nc.tensor.matmul(psum, lo, x_hi, start=False, stop=last)

        def ffn_pe(pe, f, norm, c, first=False, last=False):
            for i in range(STEPS):
                t, n = divmod(i, NS)
                cols = slice(n * BANK, (n + 1) * BANK)
                for part, (done, scaled) in enumerate(((gate_done, gate_scaled), (up_done, up_scaled))):
                    psum = banks[:, 2 * (i % 2) + part, :]
                    if i >= 2:
                        pe.wait_ge(scaled, STEPS * c + i - 1)
                    elif i == 0 and not first:
                        pe.wait_ge(scaled, STEPS * c)
                    for k in range(KT):
                        u = 2 * part + k // 4
                        if i == 0 and k % 4 == 0:
                            pe.wait_ge(w_ready[u], c + 1)
                        if first and t == 0 and part == 0:
                            pe.wait_ge(hn_ready, norm.tiles + n * KT + k + 1)
                        w = slice((k % 4) * FC + t * P, (k % 4) * FC + (t + 1) * P)
                        mm = three(psum, whi(u)[:, w], wlo(u)[:, w], hn_hi[:, k, cols], hn_lo[:, k, cols],
                                   k == 0, k == KT - 1)
                    mm.then_inc(done, 1)
                if first and i < NS:
                    stat_pe(pe, norm, i)
            for j in range(OUTS):
                n, m = divmod(j, KT)
                cols = slice(n * BANK, (n + 1) * BANK)
                if j % KT == 0:
                    pe.wait_ge(hid_ready, STEPS * c + 3 + n)
                if j >= 4:
                    pe.wait_ge(x_updated, OUTS * c + j - 3)
                elif j == 0 and not first:
                    pe.wait_ge(x_updated, OUTS * c)
                for t in range(2):
                    if j == 0:
                        pe.wait_ge(w_ready[4 + t], c + 1)
                    w = slice(m * P, (m + 1) * P)
                    mm = three(banks[:, 4 + j % 4, :], whi(4 + t)[:, w], wlo(4 + t)[:, w],
                               hid_hi[:, t, cols], hid_lo[:, t, cols], t == 0, t == 1)
                mm.then_inc(down_done, 1)
                if last and j == Y_FIRST:
                    y_stat_pe(pe, 0)
                if last and j == Y_FIRST + 1:
                    y_turn_pe(pe, 0)
            if last:
                y_stat_pe(pe, 1)

        Y_FIRST = 11

        def y_act(act, j):
            n, kt = divmod(j, KT)
            cols = slice(n * BANK, (n + 1) * BANK)
            nc.scalar.activation(y[:, n, kt, :], xT[:, kt, cols], ACT.Copy,
                                 scale=gains[:, normf.gain + kt:normf.gain + kt + 1]).then_inc(y_ready, 1)

        def y_stat_pe(pe, n):
            bank = 3 if n == 0 else 4
            pe.wait_ge(ssum_ready, normf.halves + n + 1)
            if n:
                pe.wait_ge(x_updated, OUTS * 2 * CHUNKS - 3)
            for i in range(4):
                for part in (ssum_hi, ssum_lo):
                    mm = nc.tensor.matmul(banks[:, bank, 2 * i:2 * i + 2], part[:, n, i * P:(i + 1) * P], ones[:, 0:2],
                                          start=part is ssum_hi, stop=part is ssum_lo)
            mm.then_inc(stat_ready, 1)

        def y_rstd_dve(dve, n):
            cols = slice(4 * n, 4 * n + 4)
            bank = 3 if n == 0 else 4
            dve.wait_ge(stat_ready, normf.halves + n + 1)
            nc.vector.tensor_scalar(rstd_col[:, cols], banks[:, bank, 0:8:2], 1.0 / D, EPS, ALU.mult,
                                    ALU.add).then_inc(var_ready, 1)
            dve.wait_ge(var_ready, normf.halves + n + 1)
            nc.vector.reciprocal(rstd_col[:, cols], rstd_col[:, cols]).then_inc(inv_ready, 1)

        def y_rstd_act(act, n):
            cols = slice(4 * n, 4 * n + 4)
            act.wait_ge(inv_ready, normf.halves + n + 1)
            nc.scalar.activation(rstd_col[:, cols], rstd_col[:, cols], ACT.Sqrt).then_inc(rstd_ready, 1)

        def y_turn_pe(pe, n):
            pe.wait_ge(y_ready, KT * (n + 1))
            pe.wait_ge(var_ready, normf.halves + 1)
            for b in range(4 * n, 4 * n + 4):
                for h in range(2):
                    if b >= 2:
                        pe.wait_ge(yout_dve if h else yout_act, b - 1)
                    for k in range(4):
                        mm = nc.tensor.transpose(banks[:, 2 * (b % 2) + h, k * P:(k + 1) * P],
                                                 y[:, n, 4 * h + k, (b % 4) * P:(b % 4 + 1) * P], ident[:])
                    mm.then_inc(y_turned, 1)

        def yout_half_act(act, n):
            act.wait_ge(rstd_ready, normf.halves + n + 1)
            for b in range(4 * n, 4 * n + 4):
                act.wait_ge(y_turned, 2 * b + 1)
                nc.scalar.activation(yout[:, b, 0:BANK], banks[:, 2 * (b % 2), :], ACT.Copy,
                                     scale=rstd_col[:, b:b + 1]).then_inc(yout_act, 1)

        def yout_half_dve(dve, n):
            dve.wait_ge(rstd_ready, normf.halves + n + 1)
            for b in range(4 * n, 4 * n + 4):
                dve.wait_ge(y_turned, 2 * b + 2)
                nc.vector.tensor_scalar(yout[:, b, BANK:D], banks[:, 2 * (b % 2) + 1, :], rstd_col[:, b:b + 1], None,
                                        ALU.mult).then_inc(yout_dve, 1)

        def ffn_act(act, f, norm, c, first=False, last=False):
            for u in (4, 5):
                if not first:
                    act.wait_ge(down_done, OUTS * c)
                w_split_act(act, f, c, u)
            for i in range(STEPS):
                t, n = divmod(i, NS)
                if first and i < NS:
                    rstd_act(act, norm, n)
                act.wait_ge(gate_scaled, STEPS * c + i + 1)
                nc.scalar.activation(gs[:, i % 2, :], gs[:, i % 2, :], ACT.Silu).then_inc(silu_ready, 1)
                act.wait_ge(prod_ready, STEPS * c + i + 1)
                nc.scalar.activation(hid_hi[:, t, n * BANK:(n + 1) * BANK], us[:, i % 2, :],
                                     ACT.Copy).then_inc(hid_hi_ready, 1)
            if not last:
                act.wait_ge(gate_done, STEPS * (c + 1))
                for u in (0, 1):
                    w_split_act(act, f, c + 1, u)
                act.wait_ge(up_done, STEPS * (c + 1))
                for u in (2, 3):
                    w_split_act(act, f, c + 1, u)

        def ffn_dve(dve, f, norm, c, first=False, last=False):
            for u in (4, 5):
                w_split_dve(dve, f, c, u)
            for i in range(STEPS):
                if first and i < NS:
                    rstd_dve(dve, norm, i)
                t, n = divmod(i, NS)
                cols = slice(n * BANK, (n + 1) * BANK)
                b = i % 2
                dve.wait_ge(gate_done, STEPS * c + i + 1)
                if first and i < NS:
                    dve.wait_ge(rstd_ready, norm.halves + n + 1)
                nc.vector.tensor_tensor(gs[:, b, :], banks[:, 2 * b, :], rstd[:, cols],
                                        ALU.mult).then_inc(gate_scaled, 1)
                dve.wait_ge(up_done, STEPS * c + i + 1)
                nc.vector.tensor_tensor(us[:, b, :], banks[:, 2 * b + 1, :], rstd[:, cols],
                                        ALU.mult).then_inc(up_scaled, 1)
                dve.wait_ge(up_scaled, STEPS * c + i + 1)
                dve.wait_ge(silu_ready, STEPS * c + i + 1)
                nc.vector.tensor_tensor(us[:, b, :], gs[:, b, :], us[:, b, :], ALU.mult).then_inc(prod_ready, 1)
                dve.wait_ge(hid_hi_ready, STEPS * c + i + 1)
                nc.vector.tensor_tensor(hid_lo[:, t, cols], us[:, b, :], hid_hi[:, t, cols].bitcast(F32),
                                        ALU.subtract).then_inc(hid_ready, 1)
            for j in range(OUTS):
                m, cols = halves(j)
                dve.wait_ge(down_done, OUTS * c + j + 1)
                if j == 0 and not first:
                    dve.wait_ge(x_updated, OUTS * c)
                nc.vector.scalar_tensor_tensor(out=xT[:, m, cols], in0=banks[:, 4 + j % 4, :], scalar=0.5,
                                               in1=xT[:, m, cols], op0=ALU.mult,
                                               op1=ALU.add).then_inc(x_updated, 1)
                if not last and j in (2, 5, 8, 11):
                    w_split_dve(dve, f, c + 1, j // 3)
                if last and f is ffn2 and j == Y_FIRST - 1:
                    stat_split_dve(dve, normf, 0)
                    y_rstd_dve(dve, 0)
                if last and f is ffn2 and j == Y_FIRST + 1:
                    yout_half_dve(dve, 0)

        STEPS_A = 22
        TURNS = ([("v", 0, 0)] + [(0, 0, j) for j in range(4)] + [("v", 1, 0)] + [(0, 1, j) for j in range(8)]
                 + [(1, g, j) for g in range(2) for j in range(4 * (g + 1))])
        TURNS_AT = {4: (0,), 6: (1, 2), 7: (3, 4), 8: (5,), 9: (6, 7), 10: (8, 9), 11: (10, 11), 12: (12, 13),
                    13: (14, 15), 14: (16, 17), 16: (18, 19), 17: (20, 21), 18: (22, 23), 19: (24, 25)}
        PIECES = ((0, 3), (3, 6), (6, 8))
        V_STEPS = (0, 1, 2, 3, 4, 5)
        QK_STEPS = (7, 8, 9, 10, 11, 15, 16, 17, 18, 19, 20, 21)
        UNIT_HALF = ((0, 0), (1, 0), (0, 1), (1, 1), (2, 0), (2, 1))
        SLOT1_AT = {1: 0, 2: 1, 3: 2, 5: 3}
        SLOT0_AT = {10: 0, 16: 1, 19: 2}
        W_AT = {0: 0, 2: 1, 9: 2}
        O_AT = {9: 0, 14: 1, 16: 2, 21: 3}
        TAIL_AT = {6: 0, 7: 1, 8: 2, 9: 3, 10: 4, 12: 5, 13: 6, 16: 7, 17: 8, 19: 9}
        TAIL = KT - 1 + KT

        def pair_load(sp, p, u):
            src = fox_w_in[0, :, bass.ds(u * D + p * P, P)].rearrange("(k p) n -> p k n", p=P)
            sp.dma_start(raw[:, u, :].rearrange("p (k n) -> p k n", n=P), src).then_inc(pw_loaded[u], 16)

        def pw_split_act(act, p, u):
            act.wait_ge(pw_loaded[u], 16 * (p + 1))
            nc.scalar.activation(wa_hi[:, u, :], raw[:, u, :], ACT.Copy).then_inc(pw_hi_ready[u], 1)

        def pw_split_low(eng, ops, p, u):
            eng.wait_ge(pw_hi_ready[u], p + 1)
            ops.tensor_tensor(wa_lo[:, u, :], raw[:, u, :], wa_hi[:, u, :].bitcast(F32),
                                    ALU.subtract).then_inc(pw_ready[u], 1)

        def project_pe(pe, p, idx, part, bank):
            u, n = UNIT_HALF[idx]
            if part == 0 and n == 0:
                pe.wait_ge(pw_ready[u], p + 1)
            for k in range(*PIECES[part]):
                w = slice(k * P, (k + 1) * P)
                cols = slice(n * BANK, (n + 1) * BANK)
                mm = three(banks[:, bank, :], wa_hi[:, u, w], wa_lo[:, u, w], hn_hi[:, k, cols], hn_lo[:, k, cols],
                           k == 0, k == KT - 1)
            if part == 2:
                mm.then_inc(proj_done, 1)

        def t_dve(dve, p, idx, bank):
            u, n = UNIT_HALF[idx]
            cols = slice(n * BANK, (n + 1) * BANK)
            dve.wait_ge(proj_done, 6 * p + idx + 1)
            nc.vector.scalar_tensor_tensor(out=t[:, u, cols], in0=banks[:, bank, :],
                                           scalar=-float(HD) ** -0.5 if u == 0 else 1.0, in1=rstd[:, cols],
                                           op0=ALU.mult, op1=ALU.mult).then_inc(t_ready, 1)

        def aug_act(act, p, h, idx):
            u, n = UNIT_HALF[idx]
            cols = slice(n * BANK, (n + 1) * BANK)
            rows = slice(h * HD, (h + 1) * HD)
            act.wait_ge(t_ready, 6 * p + idx + 1)
            parts, ext = (q_parts, q_ext) if u == 0 else (k_parts, k_ext)
            own = slice(HD, P) if u == 0 else slice(0, HD)
            nc.scalar.activation(ext[rows, h, cols], t[rows, u, cols], ACT.Copy).then_inc(aug_hi_ready[h], 1)
            nc.scalar.activation(parts[own, h, cols], t[rows, u, cols], ACT.Copy).then_inc(aug_hi_ready[h], 1)

        def aug_dve(dve, p, h, idx):
            u, n = UNIT_HALF[idx]
            cols = slice(n * BANK, (n + 1) * BANK)
            rows = slice(h * HD, (h + 1) * HD)
            parts, ext = (q_parts, q_ext) if u == 0 else (k_parts, k_ext)
            own = slice(0, HD) if u == 0 else slice(HD, P)
            dve.wait_ge(aug_hi_ready[h], 8 * p + 2 * idx + 2)
            nc.vector.tensor_tensor(parts[own, h, cols], t[rows, u, cols], ext[rows, h, cols].bitcast(F32),
                                    ALU.subtract).then_inc(aug_ready[h], 1)

        def probs(h, b):
            return p_low[:, b, 0:(b + 1) * P] if b < 4 else p_high[:, b - 4, 0:(b + 1) * P]

        def scores(s):
            b = s % 8
            return banks[:, 2 * (s % 2):2 * (s % 2) + 2, :].rearrange("p a n -> p (a n)")[:, 0:(b + 1) * P]

        def first_col(g, j):
            return max(0, j - 4 * g) * P

        def attend_pe(pe, p, proj):
            for s in range(STEPS_A):
                if s < 16:
                    h, b = divmod(s, 8)
                    if b % 4 == 0:
                        pe.wait_ge(aug_ready[h], 4 * p + 2 + b // 2)
                    if b == 0:
                        pe.wait_ge(ext_loaded[h], 32 * (p + 1))
                    if s >= 2:
                        pe.wait_ge(exp_ready, 16 * p + s - 1)
                    width = (b + 1) * P
                    qs = slice(b * P, (b + 1) * P)
                    rows = slice(0, HD + 4) if h == 0 else slice(0, P)
                    for c0 in range(0, width, BANK):
                        c1 = min(width, c0 + BANK)
                        psum = banks[:, 2 * (s % 2) + c0 // BANK, 0:c1 - c0]
                        diagonal = c1 == width
                        nc.tensor.matmul(psum, q_parts[:, h, qs], k_parts[:, h, c0:c1], start=True, stop=False)
                        mm = nc.tensor.matmul(psum, q_ext[rows, h, qs], k_ext[rows, h, c0:c1],
                                              start=False, stop=not diagonal)
                        if diagonal:
                            mm = nc.tensor.matmul(banks[:, 2 * (s % 2) + c0 // BANK, c1 - c0 - P:c1 - c0],
                                                  ident_r[:], mask[:], start=False, stop=True)
                    mm.then_inc(scores_done, 1)
                if s in V_STEPS:
                    i = V_STEPS.index(s)
                    if i == 0:
                        pe.wait_ge(t_ready, 6 * p + 4)
                    elif i == 3:
                        pe.wait_ge(o_ready, 4 * p + 1)
                    project_pe(pe, p, 4 + i // 3, i % 3, 7 - i // 3)
                if proj and s in QK_STEPS:
                    i = QK_STEPS.index(s)
                    if i % 3 == 0:
                        pe.wait_ge(t_ready, 6 * (p + 1) + (i // 3 if i else -1))
                    project_pe(pe, p + 1, i // 3, i % 3, 7)
                for r in TURNS_AT.get(s - 2, ()):
                    h, g, j = TURNS[r]
                    if h == "v":
                        continue
                    pe.wait_ge(part_ready, len(TURNS) * p + r + 1)
                    if j == 0:
                        pe.wait_ge(o_ready, 4 * p + 2 * h + g + 1)
                        if h == 0 and g == 0:
                            pe.wait_ge(t_ready, 6 * p + 6)
                    c0 = first_col(g, j)
                    nc.tensor.matmul(banks[:, 6, c0:BANK], v_parts[:, j, h, :, :], pt_hi[:, r % 4, c0:BANK],
                                     start=j == 0, stop=False)
                    nc.tensor.matmul(banks[:, 6, c0:BANK], v_parts[:, j, h, :, :], pt_lo[:, r % 4, c0:BANK],
                                     start=False, stop=j == 4 * g + 3).then_inc(pv_done, 1)
                for r in TURNS_AT.get(s, ()):
                    h, g, j = TURNS[r]
                    if r >= 2:
                        pe.wait_ge(part_ready, len(TURNS) * p + r - 1)
                    if h == "v":
                        pe.wait_ge(t_ready, 6 * p + 5 + g)
                        for i in range(4):
                            mm = nc.tensor.transpose(banks[:, 4 + r % 2, i * P:(i + 1) * P],
                                                     t[:, 2, g * BANK + i * P:g * BANK + (i + 1) * P], ident[:])
                    else:
                        if j == 0:
                            pe.wait_ge(p_ready, 16 * p + 8 * h + 4 * g + 4)
                        for i in range(first_col(g, j) // P, 4):
                            src = (p_high if g else p_low)[:, i, j * P:(j + 1) * P]
                            mm = nc.tensor.transpose(banks[:, 4 + r % 2, i * P:(i + 1) * P], src, ident[:])
                    mm.then_inc(turned, 1)

        def o_half_act(act, p, i):
            act.wait_ge(pv_done, 24 * p + (4, 12, 16, 24)[i])
            act.wait_ge(o_ready, 4 * p + i + 1)
            nc.scalar.activation(o_half[0:HD, :], banks[HD:P, 6, :], ACT.Copy).then_inc(o_half_ready, 1)

        def o_dve(dve, p, i):
            h, g = divmod(i, 2)
            if i == 0:
                dve.wait_ge(oT_free, 16 * (p + 1))
            dve.wait_ge(o_half_ready, 4 * p + i + 1)
            nc.vector.tensor_tensor(oT[h * HD:(h + 1) * HD, g * BANK:(g + 1) * BANK], banks[0:HD, 6, :],
                                    o_half[0:HD, :], ALU.add).then_inc(o_ready, 1)

        def attend_act(act, p, proj):
            for s in range(STEPS_A):
                for r in TURNS_AT.get(s - 1, ()):
                    h, g, j = TURNS[r]
                    act.wait_ge(turned, len(TURNS) * p + r + 1)
                    if h == "v":
                        nc.scalar.activation(v_parts[:, 4 * g:4 * g + 4, :, 0, :],
                                             banks[:, 4 + r % 2, :].rearrange("p (j h d) -> p j h d", j=4, h=2),
                                             ACT.Copy).then_inc(part_hi_ready, 1)
                    else:
                        c0 = first_col(g, j)
                        nc.scalar.activation(pt_hi[:, r % 4, c0:BANK], banks[:, 4 + r % 2, c0:BANK],
                                             ACT.Copy).then_inc(part_hi_ready, 1)
                if s - 1 in O_AT:
                    o_half_act(act, p, O_AT[s - 1])
                if s == 0:
                    aug_act(act, p, 0, 3)
                if s in SLOT1_AT:
                    aug_act(act, p, 1, SLOT1_AT[s])
                if proj and s in SLOT0_AT:
                    aug_act(act, p + 1, 0, SLOT0_AT[s])
                if s < 16:
                    if s == 12:
                        act.wait_ge(turned, len(TURNS) * p + 14)
                    act.wait_ge(low_ready, 16 * p + s + 1)
                    nc.scalar.activation(probs(s // 8, s % 8), scores(s), ACT.Exp, bias=low[:, s:s + 1], scale=-1.0,
                                         accum_out=rsum[:, s:s + 1]).then_inc(exp_ready, 1)
                if proj and s in W_AT:
                    pw_split_act(act, p + 1, W_AT[s])
                if not proj and s in TAIL_AT:
                    tail_act(act, TAIL_AT[s])
            o_half_act(act, p, 3)

        def attend_dve(dve, p, proj):
            for s in range(STEPS_A):
                for r in TURNS_AT.get(s - 1, ()):
                    h, g, j = TURNS[r]
                    dve.wait_ge(part_hi_ready, len(TURNS) * p + r + 1)
                    if h == "v":
                        for head in range(2):
                            v = nc.vector.tensor_tensor(
                                v_parts[:, 4 * g:4 * g + 4, head, 1, :],
                                banks[:, 4 + r % 2, :].rearrange("p (j h d) -> p j h d", j=4, h=2)[:, :, head, :],
                                v_parts[:, 4 * g:4 * g + 4, head, 0, :].bitcast(F32), ALU.subtract)
                        v.then_inc(part_ready, 1)
                    else:
                        c0 = first_col(g, j)
                        nc.vector.tensor_tensor(pt_lo[:, r % 4, c0:BANK], banks[:, 4 + r % 2, c0:BANK],
                                                pt_hi[:, r % 4, c0:BANK].bitcast(F32),
                                                ALU.subtract).then_inc(part_ready, 1)
                if s < 16:
                    dve.wait_ge(scores_done, 16 * p + s + 1)
                    nc.vector.tensor_reduce(low[:, s:s + 1], scores(s), AX_X, ALU.min).then_inc(low_ready, 1)
                if s - 1 in O_AT:
                    o_dve(dve, p, O_AT[s - 1])
                if 1 <= s <= 16:
                    dve.wait_ge(exp_ready, 16 * p + s)
                    nc.vector.reciprocal(rinv[:, s - 1:s], rsum[:, s - 1:s]).then_inc(rinv_ready, 1)
                    dve.wait_ge(rinv_ready, 16 * p + s)
                    pr = probs((s - 1) // 8, (s - 1) % 8)
                    nc.vector.tensor_scalar(pr, pr, rinv[:, s - 1:s], None, ALU.mult).then_inc(p_ready, 1)
                if s == 0:
                    aug_dve(dve, p, 0, 3)
                if s in SLOT1_AT:
                    aug_dve(dve, p, 1, SLOT1_AT[s])
                if proj and s in SLOT0_AT:
                    aug_dve(dve, p + 1, 0, SLOT0_AT[s])
                if s in V_STEPS[2::3]:
                    t_dve(dve, p, 4 + V_STEPS.index(s) // 3, 7 - V_STEPS.index(s) // 3)
                if proj and s in QK_STEPS[2::3]:
                    t_dve(dve, p + 1, QK_STEPS.index(s) // 3, 7)
                if not proj and s in TAIL_AT:
                    tail_dve(dve, TAIL_AT[s])
            o_dve(dve, p, 3)

        def attend_pool(pool, p, proj):
            for s in range(16):
                if proj and s in W_AT:
                    pw_split_low(pool, nc.gpsimd, p + 1, W_AT[s])
                if proj and s % 8 == 7:
                    pool.wait_ge(scores_done, 16 * p + s + 1)
                    ext_load(pool, p + 1, s // 8)
            if proj:
                pool.wait_ge(o_ready, 4 * (p + 1) + 1)
                pool.dma_start(o_dram[bass.ds(p, 1), :, :].rearrange("a p s -> (a p) s"), oT[:]).then_inc(oT_free, 16)

        def ext_load(pool, p, h):
            r = HD if h == 0 else 0
            for dst, a in ((k_ext[r:r + 2, h, :], 0), (q_ext[r + 2:r + 4, h, :], 2)):
                pool.dma_start(dst, ext_dram[bass.ds(2 * p + h, 1), a:a + 2, :].rearrange("h a s -> (h a) s")
                               ).then_inc(ext_loaded[h], 16)

        def tail_place(e):
            if e < KT - 1:
                return hn_hi[:, e, :], hn_lo[:, e, :]
            return wo_unit(e - (KT - 1))

        def wo_unit(m):
            return (wa_hi[:, m, :], wa_lo[:, m, :]) if m < 3 else (wo_hi[:, m - 3, :], wo_lo[:, m - 3, :])

        def tail_sync(sp):
            for e in range(TAIL):
                if e < RAW:
                    sp.wait_ge(pw_ready[e], PAIRS)
                else:
                    sp.wait_ge(tail_ready, e - RAW + 1)
                slot = raw[:, e % RAW, :]
                if e < KT - 1:
                    sp.wait_ge(oT_free, 16 * (e + 2))
                    sp.dma_start(slot, o_dram[e]).then_inc(tail_loaded[e % RAW], 16)
                else:
                    m = e - (KT - 1)
                    sp.dma_start(slot.rearrange("p (k n) -> p k n", n=P),
                                 fox_w_o[0, :, m * P:(m + 1) * P].rearrange("(k p) n -> p k n", p=P)
                                 ).then_inc(tail_loaded[e % RAW], 16)

        def tail_act(act, e):
            act.wait_ge(tail_loaded[e % RAW], 16 * (e // RAW + 1))
            nc.scalar.activation(tail_place(e)[0], raw[:, e % RAW, :], ACT.Copy).then_inc(tail_hi_ready, 1)

        def tail_dve(dve, e):
            dve.wait_ge(tail_hi_ready, e + 1)
            hi, lo = tail_place(e)
            nc.vector.tensor_tensor(lo, raw[:, e % RAW, :], hi.bitcast(F32), ALU.subtract).then_inc(tail_ready, 1)

        def wo_pe(pe):
            for j in range(OUTS):
                n, m = divmod(j, KT)
                cols = slice(n * BANK, (n + 1) * BANK)
                if n == 0:
                    pe.wait_ge(tail_ready, KT + m)
                if j >= 4:
                    pe.wait_ge(wo_added, j - 3)
                hi, lo = wo_unit(m)
                for k in range(KT):
                    if j == 0 and k == KT - 1:
                        pe.wait_ge(o7_ready, 1)
                    w = slice(k * P, (k + 1) * P)
                    mm = three(banks[:, 4 + j % 4, :], hi[:, w], lo[:, w], hn_hi[:, k, cols], hn_lo[:, k, cols],
                               k == 0, k == KT - 1)
                mm.then_inc(wo_done, 1)

        block = ctx.enter_context(nc.Block())

        @block.sync
        def _(sp):
            for b in range(SB):
                sp.dma_start(xin[:, b, :], x[0, b * P:(b + 1) * P, :]).then_inc(x_loaded[b], 16)
                if b == 3:
                    for u in range(2):
                        ffn_load(sp, ffn1, 0, u)
            ffn_load(sp, ffn1, 0, 2)
            ffn_sync(sp, ffn1)
            for u in range(RAW):
                sp.wait_ge(w_ready[u + RAW], CHUNKS)
                pair_load(sp, 0, u)
            for kt in range(KT):
                sp.wait_ge(x_updated, OUTS * (CHUNKS - 1) + KT + kt + 1)
                sp.dma_start(x_dram[kt], xT[:, kt, :]).then_inc(x_spilled, 16)
            with sp.Fori(0, PAIRS - 1) as p:
                for u in range(3):
                    sp.wait_ge(pw_ready[u], p + 1)
                    pair_load(sp, p + 1, u)
            tail_sync(sp)
            for u in range(RAW):
                sp.wait_ge(tail_ready, TAIL - RAW + u + 1)
                ffn_load(sp, ffn2, CHUNKS, u)
            ffn_sync(sp, ffn2)
            for b in range(SB):
                sp.wait_ge(yout_act, b + 1)
                sp.wait_ge(yout_dve, b + 1)
                sp.dma_start(out[0, b * P:(b + 1) * P, :], yout[:, b, :]).then_inc(stored, 16)
            sp.wait_ge(stored, 16 * SB)

        @block.gpsimd
        def _(pool):
            for i, g in enumerate((norm_ffn1[0, :], norm_mix[0, :], norm_ffn2[0, :], norm_final)):
                pool.dma_start(gain_rows[i * KT:(i + 1) * KT, :],
                               g.rearrange("(k p) -> k p", p=P)).then_inc(gains_loaded, 16)
            nc.gpsimd.memset(ident[:], 0.0).then_inc(ident_made, 1)
            pool.wait_ge(ident_made, 1)
            nc.gpsimd.affine_select(out=ident[:], in_=ident[:], compare_op=ALU.not_equal, fill=1.0, base=0,
                                    pattern=[[-1, P]], channel_multiplier=1).then_inc(ident_made, 1)
            pool.dma_start(b_f[:], fox_b_f.rearrange("a h -> h a")).then_inc(gate_in_loaded, 16)
            pool.dma_start(wf_raw[:], fox_w_in[0, :, 3 * D:3 * D + NH].rearrange("(k p) n -> p k n", p=P)
                           ).then_inc(gate_in_loaded, 16)
            nc.gpsimd.memset(mask0[:], 0.0).then_inc(mask_made, 1)
            pool.wait_ge(mask_made, 1)
            nc.gpsimd.affine_select(out=mask0[:], in_=mask0[:], compare_op=ALU.is_ge, fill=1e38, base=0,
                                    pattern=[[-1, P]], channel_multiplier=1).then_inc(mask_made, 1)
            norm_pool(pool, norm1)
            norm_pool(pool, norm2)
            pool.wait_ge(f_step, 8)
            pool.dma_start(ext_dram, ext_rows[:]).then_inc(oT_free, 16)
            pool.wait_ge(oT_free, 16)
            pool.wait_ge(rows_one, 4)
            for h in range(2):
                ext_load(pool, 0, h)
            with pool.Fori(0, PAIRS - 1) as p:
                attend_pool(pool, p, True)
            pool.wait_ge(scores_done, 16 * PAIRS)
            for kt in range(KT):
                pool.dma_start(xT[:, kt, :], x_dram[kt]).then_inc(x_back[kt], 16)
            norm_pool(pool, norm3)
            norm_pool(pool, normf)

        @block.tensor
        def _(pe):
            pe.wait_ge(ident_made, 2)
            for b in range(SB):
                pe.wait_ge(x_loaded[b], 16)
                for h in range(2):
                    if b >= 4:
                        pe.wait_ge(x_kept_dve if h else x_kept_act, b - 3)
                    for i in range(4):
                        mm = nc.tensor.transpose(banks[:, 2 * (b % 4) + h, i * P:(i + 1) * P],
                                                 xin[:, b, (4 * h + i) * P:(4 * h + i + 1) * P], ident[:])
                    mm.then_inc(x_turned, 1)
                if b == 1:
                    pe.wait_ge(gains_loaded, 64)
                    nc.tensor.transpose(banks[:, 7, 0:4 * KT], gain_rows[:],
                                        ident[0:4 * KT, 0:4 * KT]).then_inc(gains_turned, 1)
                if b == 2:
                    pe.wait_ge(gains_ready, 1)
            pe.wait_ge(x_kept_act, SB)
            pe.wait_ge(x_kept_dve, SB)
            pe.wait_ge(ones_made, 1)
            ffn_pe(pe, ffn1, norm1, 0, first=True)
            with pe.Fori(1, CHUNKS) as c:
                ffn_pe(pe, ffn1, norm1, c)
            for n in range(NS):
                cols = slice(n * BANK, (n + 1) * BANK)
                if n == 0:
                    pe.wait_ge(wf_ready, 1)
                for k in range(KT):
                    pe.wait_ge(hn_ready, norm2.tiles + n * KT + k + 1)
                    mm = three(banks[0:NH, 6 + n, :], wf_hi[:, k, :], wf_lo[:, k, :], hn_hi[:, k, cols],
                               hn_lo[:, k, cols], k == 0, k == KT - 1)
                mm.then_inc(f_done, 1)
                stat_pe(pe, norm2, n)
            for idx in range(4):
                for part in range(3):
                    project_pe(pe, 0, idx, part, idx)
            pe.wait_ge(ident_r_made, 2)
            with pe.Fori(0, PAIRS - 1) as p:
                attend_pe(pe, p, True)
            attend_pe(pe, PAIRS - 1, False)
            wo_pe(pe)
            ffn_pe(pe, ffn2, norm3, CHUNKS, first=True)
            with pe.Fori(CHUNKS + 1, 2 * CHUNKS - 1) as c:
                ffn_pe(pe, ffn2, norm3, c)
            ffn_pe(pe, ffn2, norm3, 2 * CHUNKS - 1, last=True)
            y_turn_pe(pe, 1)

        @block.scalar
        def _(act):
            def keep_act(b):
                act.wait_ge(x_turned, 2 * b + 1)
                nc.scalar.activation(xT[:, 0:4, b * P:(b + 1) * P],
                                     banks[:, 2 * (b % 4), :].rearrange("p (k s) -> p k s", k=4),
                                     ACT.Copy).then_inc(x_kept_act, 1)

            for b in range(4):
                keep_act(b)
            act.wait_ge(gains_ready, 1)
            act.wait_ge(x_kept_act, 4)
            act.wait_ge(x_kept_dve, 4)
            for i in range(4):
                norm_act(norm1, 2 * i)
                norm_act(norm1, 2 * i + 1)
                keep_act(4 + i)
                if i < 2:
                    w_split_act(act, ffn1, 0, i)
            for j in range(KT):
                square_act(act, norm1, j)
                if j in (0, 2):
                    w_split_act(act, ffn1, 0, 2 + j // 2)
            act.wait_ge(x_kept_act, SB)
            act.wait_ge(x_kept_dve, SB)
            for j in range(KT, NS * KT):
                norm_act(norm1, j)
            stat_split_act(act, norm1, 0)
            for j in range(KT, NS * KT):
                square_act(act, norm1, j)
            stat_split_act(act, norm1, 1)
            ffn_act(act, ffn1, norm1, 0, first=True)
            with act.Fori(1, CHUNKS - 1) as c:
                ffn_act(act, ffn1, norm1, c)
            ffn_act(act, ffn1, norm1, CHUNKS - 1, last=True)
            act.wait_ge(gate_in_loaded, 32)
            nc.scalar.activation(wf_hi[:], wf_raw[:], ACT.Copy).then_inc(wf_hi_ready, 1)
            act.wait_ge(up_done, STEPS * CHUNKS)
            pw_split_act(act, 0, 0)
            for j in range(NS * KT):
                act.wait_ge(x_updated, OUTS * (CHUNKS - 1) + j + 1)
                norm_act(norm2, j)
                square_act(act, norm2, j)
                if j % KT == KT - 1:
                    stat_split_act(act, norm2, j // KT)
            for n in range(NS):
                rstd_act(act, norm2, n)
            for u in (1, 2):
                pw_split_act(act, 0, u)
            act.wait_ge(f_step, 3)
            nc.scalar.activation(ez[:], z[:], ACT.Abs).then_inc(f_act, 1)
            act.wait_ge(f_act, 1)
            nc.scalar.activation(ez[:], ez[:], ACT.Exp, scale=-1.0).then_inc(f_act, 1)
            act.wait_ge(f_act, 2)
            nc.scalar.activation(ez[:], ez[:], ACT.Ln, bias=1.0).then_inc(f_act, 1)
            act.wait_ge(f_step, 5)
            nc.scalar.activation(ext_rows[:, 0, :], cum[:], ACT.Copy).then_inc(f_act, 1)
            nc.scalar.activation(ext_rows[:, 2, :], cum[:], ACT.Copy, scale=-1.0).then_inc(f_act, 1)
            act.wait_ge(x_spilled, 16 * KT)
            for idx in range(3):
                aug_act(act, 0, 0, idx)
            with act.Fori(0, PAIRS - 1) as p:
                attend_act(act, p, True)
            attend_act(act, PAIRS - 1, False)
            act.wait_ge(o_ready, 4 * PAIRS + 1)
            nc.scalar.activation(hn_hi[:, KT - 1, :], oT[:], ACT.Copy).then_inc(o7_hi_ready, 1)
            for e in range(len(TAIL_AT), TAIL):
                tail_act(act, e)
            for j in range(NS * KT):
                if j % KT == 0:
                    act.wait_ge(wo_done, KT * (j // KT + 1))
                    if j:
                        w_split_act(act, ffn2, CHUNKS, 3)
                act.wait_ge(wo_added, j + 1)
                norm_act(norm3, j)
                square_act(act, norm3, j)
                if j % KT == KT - 1:
                    stat_split_act(act, norm3, j // KT)
                if j == KT - 1:
                    act.wait_ge(wo_done, KT + 3)
                    for u in range(3):
                        w_split_act(act, ffn2, CHUNKS, u)
            ffn_act(act, ffn2, norm3, CHUNKS, first=True)
            with act.Fori(CHUNKS + 1, 2 * CHUNKS - 1) as c:
                ffn_act(act, ffn2, norm3, c)
            ffn_act(act, ffn2, norm3, 2 * CHUNKS - 1, last=True)
            act.wait_ge(up_done, STEPS * 2 * CHUNKS)
            for j in range(NS * KT):
                act.wait_ge(x_updated, OUTS * (2 * CHUNKS - 1) + j + 1)
                y_act(act, j)
                square_act(act, normf, j)
                if j == KT - 1:
                    stat_split_act(act, normf, 0)
                if j == Y_FIRST:
                    y_rstd_act(act, 0)
                if j == Y_FIRST + 1:
                    yout_half_act(act, 0)
            stat_split_act(act, normf, 1)
            y_rstd_act(act, 1)
            yout_half_act(act, 1)

        @block.vector
        def _(dve):
            nc.vector.memset(ones[:].bitcast(F32), 1.0).then_inc(ones_made, 1)
            dve.wait_ge(ident_made, 2)
            nc.vector.tensor_copy(ident_r[:], ident[:]).then_inc(ident_r_made, 1)
            dve.wait_ge(mask_made, 2)
            nc.vector.tensor_copy(mask[:], mask0[:]).then_inc(ident_r_made, 1)
            def keep_dve(b):
                dve.wait_ge(x_turned, 2 * b + 2)
                nc.vector.tensor_copy(xT[:, 4:8, b * P:(b + 1) * P],
                                      banks[:, 2 * (b % 4) + 1, :].rearrange("p (k s) -> p k s", k=4)
                                      ).then_inc(x_kept_dve, 1)

            for b in range(2):
                keep_dve(b)
            dve.wait_ge(gains_turned, 1)
            nc.vector.tensor_copy(gains[:], banks[:, 7, 0:4 * KT]).then_inc(gains_ready, 1)
            for b in range(2, 4):
                keep_dve(b)
            dve.wait_ge(gains_ready, 1)
            for i in range(4):
                norm_dve(dve, norm1, 2 * i)
                norm_dve(dve, norm1, 2 * i + 1)
                keep_dve(4 + i)
                if i < 2:
                    w_split_dve(dve, ffn1, 0, i)
            for u in (2, 3):
                w_split_dve(dve, ffn1, 0, u)
            for j in range(KT, NS * KT):
                norm_dve(dve, norm1, j)
            for n in range(NS):
                stat_split_dve(dve, norm1, n)
            ffn_dve(dve, ffn1, norm1, 0, first=True)
            with dve.Fori(1, CHUNKS - 1) as c:
                ffn_dve(dve, ffn1, norm1, c)
            ffn_dve(dve, ffn1, norm1, CHUNKS - 1, last=True)
            dve.wait_ge(wf_hi_ready, 1)
            nc.vector.tensor_tensor(wf_lo[:], wf_raw[:], wf_hi[:].bitcast(F32), ALU.subtract).then_inc(wf_ready, 1)
            pw_split_low(dve, nc.vector, 0, 0)
            for n in range(NS):
                for j in range(n * KT, (n + 1) * KT):
                    norm_dve(dve, norm2, j)
                stat_split_dve(dve, norm2, n)
            for n in range(NS):
                rstd_dve(dve, norm2, n)
            for u in (1, 2):
                pw_split_low(dve, nc.vector, 0, u)
            for n in range(NS):
                cols = slice(n * BANK, (n + 1) * BANK)
                dve.wait_ge(f_done, n + 1)
                dve.wait_ge(rstd_ready, norm2.halves + n + 1)
                nc.vector.tensor_tensor(z[:, cols], banks[0:NH, 6 + n, :], rstd[0:NH, cols],
                                        ALU.mult).then_inc(f_step, 1)
            dve.wait_ge(f_step, 2)
            nc.vector.tensor_scalar(z[:], z[:], b_f[:], None, ALU.add).then_inc(f_step, 1)
            dve.wait_ge(f_act, 3)
            nc.vector.scalar_tensor_tensor(out=z[:], in0=z[:], scalar=0.0, in1=ez[:], op0=ALU.min,
                                           op1=ALU.subtract).then_inc(f_step, 1)
            dve.wait_ge(f_step, 4)
            nc.vector.tensor_tensor_scan(cum[:], ones[0:NH, 0:1].bitcast(F32).to_broadcast([NH, S]), z[:], 0.0,
                                         ALU.mult, ALU.add).then_inc(f_step, 1)
            dve.wait_ge(f_step, 5)
            dve.wait_ge(f_act, 5)
            nc.vector.tensor_tensor(ext_rows[:, 1, :], cum[:], ext_rows[:, 0, :].bitcast(F32),
                                    ALU.subtract).then_inc(f_step, 1)
            dve.wait_ge(f_step, 6)
            nc.vector.tensor_scalar(ext_rows[:, 3, :], ext_rows[:, 1, :].bitcast(F32), -1.0, None,
                                    ALU.mult).then_inc(f_step, 2)
            for idx in range(4):
                t_dve(dve, 0, idx, idx)
            dve.wait_ge(x_spilled, 16 * KT)
            for ext in (k_ext, q_ext):
                nc.vector.memset(ext[0:HD, 1, :].bitcast(F32), 0.0).then_inc(rows_zero, 1)
            dve.wait_ge(rows_zero, 2)
            for ext in (k_ext, q_ext):
                nc.vector.memset(ext[HD:HD + 4, 0, :].bitcast(F32), 1.0).then_inc(rows_one, 1)
                nc.vector.memset(ext[0:4, 1, :].bitcast(F32), 1.0).then_inc(rows_one, 1)
            for idx in range(3):
                aug_dve(dve, 0, 0, idx)
            nc.vector.tensor_copy(rinv[:], rstd[:, 0:16]).then_inc(o_ready, 1)
            with dve.Fori(0, PAIRS - 1) as p:
                attend_dve(dve, p, True)
            attend_dve(dve, PAIRS - 1, False)
            dve.wait_ge(o7_hi_ready, 1)
            nc.vector.tensor_tensor(hn_lo[:, KT - 1, :], oT[:], hn_hi[:, KT - 1, :].bitcast(F32),
                                    ALU.subtract).then_inc(o7_ready, 1)
            for e in range(len(TAIL_AT), TAIL):
                tail_dve(dve, e)
            for j in range(NS * KT):
                m, cols = halves(j)
                dve.wait_ge(wo_done, j + 1)
                if j < KT:
                    dve.wait_ge(x_back[j], 16)
                nc.vector.tensor_tensor(xT[:, m, cols], banks[:, 4 + j % 4, :], xT[:, m, cols],
                                        ALU.add).then_inc(wo_added, 1)
                if j >= KT:
                    norm_dve(dve, norm3, j - KT)
            stat_split_dve(dve, norm3, 0)
            for u in range(4):
                w_split_dve(dve, ffn2, CHUNKS, u)
            for j in range(KT, NS * KT):
                norm_dve(dve, norm3, j)
            stat_split_dve(dve, norm3, 1)
            ffn_dve(dve, ffn2, norm3, CHUNKS, first=True)
            with dve.Fori(CHUNKS + 1, 2 * CHUNKS - 1) as c:
                ffn_dve(dve, ffn2, norm3, c)
            ffn_dve(dve, ffn2, norm3, 2 * CHUNKS - 1, last=True)
            stat_split_dve(dve, normf, 1)
            y_rstd_dve(dve, 1)
            yout_half_dve(dve, 1)


_INS = ["x", "norm_ffn1", "norm_mix", "norm_ffn2", "norm_final",
        "ffn1_w_gate", "ffn1_w_up", "ffn1_w_down", "ffn2_w_gate", "ffn2_w_up", "ffn2_w_down",
        "fox_w_in", "fox_b_f", "fox_w_o"]


def kernel(**inputs):
    import numpy as _np
    import concourse.bacc as _bacc
    from concourse import mybir as _mybir
    from concourse.bass_utils import run_bass_kernel_spmd as _run

    nc = _bacc.Bacc("TRN2", target_bir_lowering=False, num_devices=1)
    arrays, args = {}, []
    for name in _INS:
        a = _np.ascontiguousarray(inputs[name])
        arrays[f"in_{name}_dram"] = a
        args.append(nc.dram_tensor(f"in_{name}_dram", a.shape, _mybir.dt.from_np(a.dtype), kind="ExternalInput").ap())
    shape = arrays["in_x_dram"].shape
    args.append(nc.dram_tensor("out_dram", shape, _mybir.dt.float32, kind="ExternalOutput").ap())
    build(nc, *args)
    r = _run(nc, [arrays], core_ids=[0])
    return r.results[0]["out_dram"]
```

```python
from contextlib import ExitStack

import concourse.bass as bass
from concourse import mybir

ALU = mybir.AluOpType
ACT = mybir.ActivationFunctionType
AX_X = mybir.AxisListType.X
F32 = mybir.dt.float32
F32R = mybir.dt.float32r

P = 128
BANK = 512
KIB = 1024
EPS = 1e-6


def build(nc, x, norm_ffn1, norm_mix, norm_ffn2, norm_final,
          ffn1_w_gate, ffn1_w_up, ffn1_w_down, ffn2_w_gate, ffn2_w_up, ffn2_w_down,
          fox_w_in, fox_b_f, fox_w_o, out):
    _, S, D = x.shape
    F = ffn1_w_gate.shape[2]
    KT = D // P
    NS = S // BANK
    SB = S // P
    FC = 2 * P
    CHUNKS = F // FC
    assert F % FC == 0 and KT == 8 and NS == 2 and CHUNKS >= 3
    UNITS = 6
    RAW = 3
    STEPS = 2 * NS
    OUTS = NS * KT
    NH = fox_b_f.shape[1]
    HD = D // NH
    PAIRS = NH // 2
    assert HD == 64 and PAIRS == KT and S == 1024

    ctx = ExitStack()
    with ctx:
        def sem(name):
            return ctx.enter_context(nc.semaphore(name))

        ctx.enter_context(nc.sbuf_tensor("arena", [P, 207 * 256], F32))
        base = 16512

        def at(name, shape, dt, kib):
            return nc.alloc_sbuf_tensor_at(name, shape, dt, offset=int(base + kib * KIB))

        hn_hi = at("hn_hi", [P, KT, S], F32R, 0)
        hn_lo = at("hn_lo", [P, KT, S], F32R, 32)
        rstd = at("rstd", [P, S], F32, 64)
        raw = at("raw", [P, RAW, 1024], F32, 68)
        wa_hi = at("wa_hi", [P, 3, 1024], F32R, 80)
        wa_lo = at("wa_lo", [P, 3, 1024], F32R, 92)
        ident = at("ident", [P, P], F32, 104)
        ones = at("ones", [P, P], F32R, 104.5)
        gain_rows = at("gain_rows", [4 * KT, P], F32, 105)
        gains = at("gains", [P, 4 * KT], F32, 105.5)
        xT = at("xT", [P, KT, S], F32, 106)
        wb_hi = at("wb_hi", [P, 3, 1024], F32R, 138)
        wb_lo = at("wb_lo", [P, 3, 1024], F32R, 150)
        hid_hi = at("hid_hi", [P, 2, S], F32R, 162)
        hid_lo = at("hid_lo", [P, 2, S], F32R, 170)
        gs = at("gs", [P, 2, BANK], F32, 178)
        us = at("us", [P, 2, BANK], F32, 182)
        sq = at("sq", [P, 2, BANK], F32, 186)
        ssum = at("ssum", [P, NS, BANK], F32, 190)
        xin = at("xin", [P, SB, D], F32, 138)
        y = at("y", [P, NS, KT, BANK], F32, 0)
        yout = at("yout", [P, SB, D], F32, 32)
        rstd_col = at("rstd_col", [P, SB], F32, 206.5)

        k_parts = at("k_parts", [P, 2, S], F32R, 106)
        k_ext = at("k_ext", [P, 2, S], F32R, 114)
        q_parts = at("q_parts", [P, 2, S], F32R, 122)
        q_ext = at("q_ext", [P, 2, S], F32R, 130)
        t = at("t", [P, 3, S], F32, 138)
        v_parts = at("v_parts", [P, SB, 2, 2, HD], F32R, 150)
        p_low = at("p_low", [P, 4, BANK], F32, 158)
        p_high = at("p_high", [P, 4, S], F32, 166)
        pt_hi = at("pt_hi", [P, 4, BANK], F32R, 182)
        pt_lo = at("pt_lo", [P, 4, BANK], F32R, 190)
        oT = at("oT", [P, S], F32, 198)
        o_half = at("o_half", [P, BANK], F32, 203)
        wo_hi = at("wo_hi", [P, 5, 1024], F32R, 138)
        wo_lo = at("wo_lo", [P, 5, 1024], F32R, 158)
        z = at("z", [NH, S], F32, 158)
        ez = at("ez", [NH, S], F32, 162)
        cum = at("cum", [NH, S], F32, 166)
        ext_rows = at("ext_rows", [NH, 2, S], F32R, 170)
        ident_r = at("ident_r", [P, P], F32R, 202)
        mask = at("mask", [P, P], F32R, 202.5)
        wf_raw = at("wf_raw", [P, KT, NH], F32, 203)
        wf_hi = at("wf_hi", [P, KT, NH], F32R, 203.5)
        wf_lo = at("wf_lo", [P, KT, NH], F32R, 204)
        b_f = at("b_f", [NH, 1], F32, 205)
        low = at("low", [P, 16], F32, 205.25)
        rsum = at("rsum", [P, 16], F32, 205.5)
        rinv = at("rinv", [P, 16], F32, 205.75)
        mask0 = at("mask0", [P, P], F32, 206)
        ext_dram = nc.dram_tensor("ext_rows_scratch", [NH, 2, S], F32R, kind="Internal").ap()
        x_dram = nc.dram_tensor("x_scratch", [KT, P, S], F32, kind="Internal").ap()
        o_dram = nc.dram_tensor("o_scratch", [KT, P, S], F32, kind="Internal").ap()

        banks = ctx.enter_context(nc.psum_tensor("banks", [P, 8, BANK], F32))

        def whi(u):
            return wa_hi[:, u, :] if u < 3 else wb_hi[:, u - 3, :]

        def wlo(u):
            return wa_lo[:, u, :] if u < 3 else wb_lo[:, u - 3, :]

        gains_loaded = sem("gains_loaded")
        ident_made = sem("ident_made")
        ones_made = sem("ones_made")
        gains_turned = sem("gains_turned")
        gains_ready = sem("gains_ready")
        x_loaded = [sem(f"x_loaded{b}") for b in range(SB)]
        x_turned = sem("x_turned")
        x_squared = sem("x_squared")
        x_kept_act = sem("x_kept_act")
        x_kept_dve = sem("x_kept_dve")

        hn_hi_ready = sem("hn_hi_ready")
        hn_ready = sem("hn_ready")
        sq_ready = sem("sq_ready")
        sq_summed = sem("sq_summed")
        stat_ready = sem("stat_ready")
        var_ready = sem("var_ready")
        inv_ready = sem("inv_ready")
        rcol_ready = sem("rcol_ready")
        rstd_turned = sem("rstd_turned")
        rstd_ready = sem("rstd_ready")
        w_loaded = [sem(f"w_loaded{u}") for u in range(UNITS)]
        w_hi_ready = [sem(f"w_hi_ready{u}") for u in range(UNITS)]
        w_ready = [sem(f"w_ready{u}") for u in range(UNITS)]
        gate_done = sem("gate_done")
        up_done = sem("up_done")
        gate_scaled = sem("gate_scaled")
        up_scaled = sem("up_scaled")
        silu_ready = sem("silu_ready")
        prod_ready = sem("prod_ready")
        hid_hi_ready = sem("hid_hi_ready")
        hid_ready = sem("hid_ready")
        down_done = sem("down_done")
        x_updated = sem("x_updated")

        class Norm:
            def __init__(self, index):
                self.gain = index * KT
                self.tiles = index * NS * KT
                self.halves = index * NS
                self.sums = (index - 1) * NS * KT
                self.stats = (index - 1) * NS

        class Ffn:
            def __init__(self, start, gate, up, down):
                self.start, self.gate, self.up, self.down = start, gate, up, down

        norm1, norm2, norm3, normf = (Norm(i) for i in range(4))
        ffn1 = Ffn(0, ffn1_w_gate, ffn1_w_up, ffn1_w_down)
        ffn2 = Ffn(CHUNKS, ffn2_w_gate, ffn2_w_up, ffn2_w_down)
        assert KT * NS == OUTS
        gate_in_loaded = sem("gate_in_loaded")
        ident_r_made = sem("ident_r_made")
        mask_made = sem("mask_made")
        wf_hi_ready = sem("wf_hi_ready")
        wf_ready = sem("wf_ready")
        f_done = sem("f_done")
        f_step = sem("f_step")
        f_act = sem("f_act")
        ext_stored = sem("ext_stored")
        x_spilled = sem("x_spilled")
        rows_zero = sem("rows_zero")
        rows_one = sem("rows_one")
        ext_loaded = [sem(f"ext_loaded{h}") for h in range(2)]
        pw_loaded = [sem(f"pw_loaded{u}") for u in range(3)]
        pw_hi_ready = [sem(f"pw_hi_ready{u}") for u in range(3)]
        pw_ready = [sem(f"pw_ready{u}") for u in range(3)]
        proj_done = sem("proj_done")
        t_ready = sem("t_ready")
        aug_hi_ready = [sem(f"aug_hi_ready{h}") for h in range(2)]
        aug_ready = [sem(f"aug_ready{h}") for h in range(2)]
        scores_done = sem("scores_done")
        low_ready = sem("low_ready")
        exp_ready = sem("exp_ready")
        rinv_ready = sem("rinv_ready")
        p_ready = sem("p_ready")
        turned = sem("turned")
        part_hi_ready = sem("part_hi_ready")
        part_ready = sem("part_ready")
        pv_done = sem("pv_done")
        o_half_ready = sem("o_half_ready")
        o_ready = sem("o_ready")
        oT_free = sem("oT_free")
        tail_loaded = [sem(f"tail_loaded{i}") for i in range(RAW)]
        tail_hi_ready = sem("tail_hi_ready")
        tail_ready = sem("tail_ready")
        o7_hi_ready = sem("o7_hi_ready")
        o7_ready = sem("o7_ready")
        x_back = [sem(f"x_back{k}") for k in range(KT)]
        wo_done = sem("wo_done")
        wo_added = sem("wo_added")
        y_ready = sem("y_ready")
        y_turned = sem("y_turned")
        yout_act = sem("yout_act")
        yout_dve = sem("yout_dve")
        stored = sem("stored")

        def halves(j):
            n, kt = divmod(j, KT)
            return kt, slice(n * BANK, (n + 1) * BANK)

        def norm_act(norm, j):
            kt, cols = halves(j)
            nc.scalar.activation(hn_hi[:, kt, cols], xT[:, kt, cols], ACT.Copy,
                                 scale=gains[:, norm.gain + kt:norm.gain + kt + 1]).then_inc(hn_hi_ready, 1)

        def square_act(act, norm, j):
            kt, cols = halves(j)
            if j >= 2:
                act.wait_ge(sq_summed, norm.sums + j - 1)
            nc.scalar.activation(sq[:, j % 2, :], xT[:, kt, cols], ACT.Square).then_inc(sq_ready, 1)

        def norm_dve(dve, norm, j):
            kt, cols = halves(j)
            dve.wait_ge(hn_hi_ready, norm.tiles + j + 1)
            nc.vector.scalar_tensor_tensor(
                out=hn_lo[:, kt, cols], in0=xT[:, kt, cols], scalar=gains[:, norm.gain + kt:norm.gain + kt + 1],
                in1=hn_hi[:, kt, cols].bitcast(F32), op0=ALU.mult, op1=ALU.subtract).then_inc(hn_ready, 1)

        def norm_pool(pool, norm):
            for j in range(NS * KT):
                n, kt = divmod(j, KT)
                pool.wait_ge(sq_ready, norm.sums + j + 1)
                if kt == 0:
                    nc.gpsimd.tensor_copy(ssum[:, n, :], sq[:, j % 2, :]).then_inc(sq_summed, 1)
                else:
                    pool.wait_ge(sq_summed, norm.sums + j)
                    nc.gpsimd.tensor_tensor(ssum[:, n, :], ssum[:, n, :], sq[:, j % 2, :],
                                            ALU.add).then_inc(sq_summed, 1)

        def stat_pe(pe, norm, n, bank):
            pe.wait_ge(sq_summed, norm.sums + KT * (n + 1))
            for i in range(4):
                mm = nc.tensor.matmul(banks[:, bank, 2 * i:2 * i + 2], ssum[:, n, i * P:(i + 1) * P],
                                      ones[:, 0:2].bitcast(F32), start=True, stop=True)
            mm.then_inc(stat_ready, 1)

        def rcol_dve(dve, norm, n, bank):
            cols = slice(4 * n, 4 * n + 4)
            if norm is norm1:
                dve.wait_ge(x_squared, 4 * (n + 1))
                sums = rstd_col[:, cols]
            else:
                dve.wait_ge(stat_ready, norm.stats + n + 1)
                sums = banks[:, bank, 0:8:2]
            nc.vector.tensor_scalar(rstd_col[:, cols], sums, 1.0 / D, EPS, ALU.mult, ALU.add).then_inc(var_ready, 1)
            dve.wait_ge(var_ready, norm.halves + n + 1)
            nc.vector.reciprocal(rstd_col[:, cols], rstd_col[:, cols]).then_inc(inv_ready, 1)

        def rcol_act(act, norm, n):
            cols = slice(4 * n, 4 * n + 4)
            act.wait_ge(inv_ready, norm.halves + n + 1)
            nc.scalar.activation(rstd_col[:, cols], rstd_col[:, cols], ACT.Sqrt).then_inc(rcol_ready, 1)

        def rstd_pe(pe, norm, n):
            pe.wait_ge(rcol_ready, norm.halves + n + 1)
            for i in range(4):
                mm = nc.tensor.transpose(banks[:, 4 + n, i * P:(i + 1) * P],
                                         rstd_col[:, 4 * n + i:4 * n + i + 1].to_broadcast([P, P]), ident[:])
            mm.then_inc(rstd_turned, 1)

        def rstd_act(act, norm, n):
            if norm is not norm1:
                rcol_act(act, norm, n)
            act.wait_ge(rstd_turned, norm.halves + n + 1)
            nc.scalar.activation(rstd[:, n * BANK:(n + 1) * BANK], banks[:, 4 + n, :], ACT.Copy
                                 ).then_inc(rstd_ready, 1)

        def ffn_load(sp, f, c, u):
            at_chunk = (c - f.start) * FC
            dst = raw[:, u % RAW, :]
            if u < 4:
                w = f.gate if u < 2 else f.up
                half = (u % 2) * (D // 2)
                src = w[0, half:half + D // 2, bass.ds(at_chunk, FC)].rearrange("(k p) n -> p k n", p=P)
                dst = dst.rearrange("p (k n) -> p k n", n=FC)
            else:
                src = f.down[0, bass.ds(at_chunk + (u - 4) * P, P), :]
            sp.dma_start(dst, src).then_inc(w_loaded[u], 16)

        def ffn_sync(sp, f, u_first=RAW):
            for u in range(u_first, UNITS):
                sp.wait_ge(w_ready[u - RAW], f.start + 1)
                ffn_load(sp, f, f.start, u)
            with sp.Fori(f.start + 1, f.start + CHUNKS) as c:
                for u in range(UNITS):
                    if u >= RAW:
                        sp.wait_ge(w_ready[u - RAW], c + 1)
                    else:
                        sp.wait_ge(w_ready[u + RAW], c)
                    ffn_load(sp, f, c, u)

        def w_split_act(act, f, c, u):
            act.wait_ge(w_loaded[u], 16 * (c + 1))
            nc.scalar.activation(whi(u), raw[:, u % RAW, :], ACT.Copy).then_inc(w_hi_ready[u], 1)

        def w_split_dve(dve, f, c, u):
            dve.wait_ge(w_hi_ready[u], c + 1)
            nc.vector.tensor_tensor(wlo(u), raw[:, u % RAW, :], whi(u).bitcast(F32),
                                    ALU.subtract).then_inc(w_ready[u], 1)

        def three(psum, hi, lo, x_hi, x_lo, first, last):
            nc.tensor.matmul(psum, hi, x_lo, start=first, stop=False)
            nc.tensor.matmul(psum, hi, x_hi, start=False, stop=False)
            return nc.tensor.matmul(psum, lo, x_hi, start=False, stop=last)

        X_TURN_AT = {(0, 0, 6): 4, (0, 0, 7): 5, (0, 1, 3): 6, (0, 1, 5): 7}
        STAT_AT = {(1, 0, 7): 0, (2, 0, 6): 1}
        RSTD_AT = {norm1: {(1, 1, 3): 0, (1, 1, 7): 1}, norm3: {(1, 1, 4): 0, (2, 1, 3): 1}}

        def x_turn_pe(pe, b):
            bank = 2 * b if b < 4 else 4 + 2 * (b % 2)
            pe.wait_ge(x_loaded[b], 16)
            for h in range(2):
                if b >= 4:
                    pe.wait_ge(x_kept_dve if h else x_kept_act, b - 1)
                for i in range(4):
                    mm = nc.tensor.transpose(banks[:, bank + h, i * P:(i + 1) * P],
                                             xin[:, b, (4 * h + i) * P:(4 * h + i + 1) * P], ident[:])
                mm.then_inc(x_turned, 1)

        def ffn_pe(pe, f, norm, c, first=False, last=False):
            for i in range(STEPS):
                t, n = divmod(i, NS)
                cols = slice(n * BANK, (n + 1) * BANK)
                for part, (done, scaled) in enumerate(((gate_done, gate_scaled), (up_done, up_scaled))):
                    psum = banks[:, 2 * (i % 2) + part, :]
                    if i >= 2:
                        pe.wait_ge(scaled, STEPS * c + i - 1)
                    elif i == 0 and not first:
                        pe.wait_ge(scaled, STEPS * c)
                    for k in range(KT):
                        u = 2 * part + k // 4
                        if i == 0 and k % 4 == 0:
                            pe.wait_ge(w_ready[u], c + 1)
                        if first and t == 0 and part == 0:
                            pe.wait_ge(hn_ready, norm.tiles + n * KT + k + 1)
                        w = slice((k % 4) * FC + t * P, (k % 4) * FC + (t + 1) * P)
                        mm = three(psum, whi(u)[:, w], wlo(u)[:, w], hn_hi[:, k, cols], hn_lo[:, k, cols],
                                   k == 0, k == KT - 1)
                        if k == KT - 1:
                            mm.then_inc(done, 1)
                        if first and norm is norm1 and (i, part, k) in X_TURN_AT:
                            x_turn_pe(pe, X_TURN_AT[i, part, k])
                        if first and norm is norm3 and (i, part, k) in STAT_AT:
                            n_stat = STAT_AT[i, part, k]
                            stat_pe(pe, norm, n_stat, 4 + n_stat)
                        if first and (i, part, k) in RSTD_AT[norm]:
                            rstd_pe(pe, norm, RSTD_AT[norm][i, part, k])
            for j in range(OUTS):
                n, m = divmod(j, KT)
                cols = slice(n * BANK, (n + 1) * BANK)
                if j % KT == 0:
                    pe.wait_ge(hid_ready, STEPS * c + 3 + n)
                if j >= 4:
                    pe.wait_ge(x_updated, OUTS * c + j - 3)
                elif j == 0 and not first:
                    pe.wait_ge(x_updated, OUTS * c)
                for t in range(2):
                    if j == 0:
                        pe.wait_ge(w_ready[4 + t], c + 1)
                    w = slice(m * P, (m + 1) * P)
                    mm = three(banks[:, 4 + j % 4, :], whi(4 + t)[:, w], wlo(4 + t)[:, w],
                               hid_hi[:, t, cols], hid_lo[:, t, cols], t == 0, t == 1)
                mm.then_inc(down_done, 1)
                if last and j == Y_FIRST:
                    stat_pe(pe, normf, 0, Y_BANK[0])
                if last and j == Y_FIRST + 1:
                    y_turn_pe(pe, 0)
                    y_turn_pe(pe, 1)
                if last and j == Y_FIRST + 3:
                    y_turn_pe(pe, 2)
                    y_turn_pe(pe, 3)
            if last:
                y_turn_pe(pe, 4)
                pe.wait_ge(x_updated, OUTS * 2 * CHUNKS - 3)
                stat_pe(pe, normf, 1, Y_BANK[1])

        Y_BANK = (3, 4)
        Y_FIRST = 11

        def y_act(act, j):
            n, kt = divmod(j, KT)
            cols = slice(n * BANK, (n + 1) * BANK)
            nc.scalar.activation(y[:, n, kt, :], xT[:, kt, cols], ACT.Copy,
                                 scale=gains[:, normf.gain + kt:normf.gain + kt + 1]).then_inc(y_ready, 1)

        YOUT_BANKS = ((0, 1), (2, 3), (0, 1), (2, 3), (0, 1), (2, 3), (5, 6), (7, 0))

        def y_turn_pe(pe, b):
            n = b // 4
            pe.wait_ge(y_ready, KT * (n + 1))
            if b == 1:
                pe.wait_ge(var_ready, normf.halves + 1)
            for h in range(2):
                if 2 <= b < 6:
                    pe.wait_ge(yout_dve if h else yout_act, b - 1)
                if b == 7 and h == 1:
                    pe.wait_ge(yout_act, 5)
                for k in range(4):
                    mm = nc.tensor.transpose(banks[:, YOUT_BANKS[b][h], k * P:(k + 1) * P],
                                             y[:, n, 4 * h + k, (b % 4) * P:(b % 4 + 1) * P], ident[:])
                mm.then_inc(y_turned, 1)

        def yout_block_act(act, b):
            act.wait_ge(rcol_ready, normf.halves + b // 4 + 1)
            act.wait_ge(y_turned, 2 * b + 1)
            nc.scalar.activation(yout[:, b, 0:BANK], banks[:, YOUT_BANKS[b][0], :], ACT.Copy,
                                 scale=rstd_col[:, b:b + 1]).then_inc(yout_act, 1)

        def yout_block_dve(dve, b):
            dve.wait_ge(rcol_ready, normf.halves + b // 4 + 1)
            dve.wait_ge(y_turned, 2 * b + 2)
            nc.vector.tensor_scalar(yout[:, b, BANK:D], banks[:, YOUT_BANKS[b][1], :], rstd_col[:, b:b + 1], None,
                                    ALU.mult).then_inc(yout_dve, 1)

        def ffn_act(act, f, norm, c, first=False, last=False):
            for u in (4, 5):
                if not first:
                    act.wait_ge(down_done, OUTS * c)
                w_split_act(act, f, c, u)
            for i in range(STEPS):
                t, n = divmod(i, NS)
                if first and i < NS:
                    rstd_act(act, norm, n)
                act.wait_ge(gate_scaled, STEPS * c + i + 1)
                nc.scalar.activation(gs[:, i % 2, :], gs[:, i % 2, :], ACT.Silu).then_inc(silu_ready, 1)
                act.wait_ge(prod_ready, STEPS * c + i + 1)
                nc.scalar.activation(hid_hi[:, t, n * BANK:(n + 1) * BANK], us[:, i % 2, :],
                                     ACT.Copy).then_inc(hid_hi_ready, 1)
            if not last:
                act.wait_ge(gate_done, STEPS * (c + 1))
                for u in (0, 1):
                    w_split_act(act, f, c + 1, u)
                act.wait_ge(up_done, STEPS * (c + 1))
                for u in (2, 3):
                    w_split_act(act, f, c + 1, u)

        def ffn_dve(dve, f, norm, c, first=False, last=False):
            for u in (4, 5):
                w_split_dve(dve, f, c, u)
            for i in range(STEPS):
                if first and i < NS and norm is not norm1:
                    rcol_dve(dve, norm, i, 4 + i)
                t, n = divmod(i, NS)
                cols = slice(n * BANK, (n + 1) * BANK)
                b = i % 2
                dve.wait_ge(gate_done, STEPS * c + i + 1)
                if first and i < NS:
                    dve.wait_ge(rstd_ready, norm.halves + n + 1)
                nc.vector.tensor_tensor(gs[:, b, :], banks[:, 2 * b, :], rstd[:, cols],
                                        ALU.mult).then_inc(gate_scaled, 1)
                dve.wait_ge(up_done, STEPS * c + i + 1)
                nc.vector.tensor_tensor(us[:, b, :], banks[:, 2 * b + 1, :], rstd[:, cols],
                                        ALU.mult).then_inc(up_scaled, 1)
                dve.wait_ge(up_scaled, STEPS * c + i + 1)
                dve.wait_ge(silu_ready, STEPS * c + i + 1)
                nc.vector.tensor_tensor(us[:, b, :], gs[:, b, :], us[:, b, :], ALU.mult).then_inc(prod_ready, 1)
                dve.wait_ge(hid_hi_ready, STEPS * c + i + 1)
                nc.vector.tensor_tensor(hid_lo[:, t, cols], us[:, b, :], hid_hi[:, t, cols].bitcast(F32),
                                        ALU.subtract).then_inc(hid_ready, 1)
            for j in range(OUTS):
                m, cols = halves(j)
                dve.wait_ge(down_done, OUTS * c + j + 1)
                if j == 0 and not first:
                    dve.wait_ge(x_updated, OUTS * c)
                nc.vector.scalar_tensor_tensor(out=xT[:, m, cols], in0=banks[:, 4 + j % 4, :], scalar=0.5,
                                               in1=xT[:, m, cols], op0=ALU.mult,
                                               op1=ALU.add).then_inc(x_updated, 1)
                if not last and j in (2, 5, 8, 11):
                    w_split_dve(dve, f, c + 1, j // 3)
                if last and f is ffn1:
                    if j in (1, 3, 5):
                        pw_split_low(dve, nc.vector, 0, j // 2)
                    if j >= KT:
                        norm_dve(dve, norm2, j - KT)
                if last and f is ffn2 and j == Y_FIRST:
                    rcol_dve(dve, normf, 0, Y_BANK[0])
                if last and f is ffn2 and j in (Y_FIRST + 1, Y_FIRST + 3):
                    for b in range(j - Y_FIRST - 1, j - Y_FIRST + 1):
                        yout_block_dve(dve, b)

        STEPS_A = 23
        TURNS = ([("v", 0, 0)] + [(0, 0, j) for j in range(4)] + [("v", 1, 0)] + [(0, 1, j) for j in range(8)]
                 + [(1, g, j) for g in range(2) for j in range(4 * (g + 1))])
        TURNS_AT = {4: (0,), 6: (1, 2), 7: (3, 4), 8: (5,), 9: (6, 7), 10: (8, 9), 11: (10, 11), 12: (12, 13),
                    14: (14, 15), 15: (16, 17), 17: (18, 19), 18: (20, 21), 19: (22, 23), 20: (24, 25)}
        PIECES = ((0, 3), (3, 6), (6, 8))
        V_STEPS = (0, 1, 2, 3, 4, 5)
        V_STEPS_LAST = (0, 1, 2, 4, 5, 6)
        QK_STEPS = (6, 7, 8, 10, 11, 12, 14, 15, 16, 18, 19, 20)
        UNIT_HALF = ((0, 0), (1, 0), (0, 1), (1, 1), (2, 0), (2, 1))
        SLOT1_AT = {1: 0, 2: 1, 3: 2, 6: 3}
        SLOT0_AT = {10: 0, 14: 1, 19: 2}
        W_AT = {0: 0, 2: 1, 10: 2}
        O_AT = {9: 0, 14: 1, 17: 2, 22: 3}
        TAIL_AT = {2: 0, 7: 1, 8: 2, 9: 3, 10: 4, 11: 5, 12: 6, 13: 7, 16: 8, 17: 9, 19: 10, 22: 11}
        TAIL = KT - 1 + KT
        FILL_AT = {9: (0, 0, 1), 10: (0, 1, 2), 11: (0, 2, 3), 12: (0, 3, 4), 14: (0, 4, 5), 15: (0, 5, 6),
                   16: (0, 6, 7), 17: (8, 0, 7), 18: (1, 0, 4), 19: (1, 4, 7), 20: (2, 0, 7), 21: (9, 0, 4),
                   22: (9, 4, 7)}
        STARTED = (0, 1, 2, 8, 9)
        WO_BANK = (7, 0, 1, 4, 5, 6, 7, 4, 2, 3, 5, 6, 7, 4, 5, 6)
        O7_AT = 20

        def pair_load(sp, p, u):
            src = fox_w_in[0, :, bass.ds(u * D + p * P, P)].rearrange("(k p) n -> p k n", p=P)
            sp.dma_start(raw[:, u, :].rearrange("p (k n) -> p k n", n=P), src).then_inc(pw_loaded[u], 16)

        def pw_split_act(act, p, u):
            act.wait_ge(pw_loaded[u], 16 * (p + 1))
            nc.scalar.activation(wa_hi[:, u, :], raw[:, u, :], ACT.Copy).then_inc(pw_hi_ready[u], 1)

        def pw_split_low(eng, ops, p, u):
            eng.wait_ge(pw_hi_ready[u], p + 1)
            ops.tensor_tensor(wa_lo[:, u, :], raw[:, u, :], wa_hi[:, u, :].bitcast(F32),
                                    ALU.subtract).then_inc(pw_ready[u], 1)

        def project_pe(pe, p, idx, part, bank):
            u, n = UNIT_HALF[idx]
            if part == 0 and n == 0:
                pe.wait_ge(pw_ready[u], p + 1)
            for k in range(*PIECES[part]):
                w = slice(k * P, (k + 1) * P)
                cols = slice(n * BANK, (n + 1) * BANK)
                mm = three(banks[:, bank, :], wa_hi[:, u, w], wa_lo[:, u, w], hn_hi[:, k, cols], hn_lo[:, k, cols],
                           k == 0, k == KT - 1)
            if part == 2:
                mm.then_inc(proj_done, 1)

        def t_dve(dve, p, idx, bank):
            u, n = UNIT_HALF[idx]
            cols = slice(n * BANK, (n + 1) * BANK)
            dve.wait_ge(proj_done, 6 * p + idx + 1)
            nc.vector.scalar_tensor_tensor(out=t[:, u, cols], in0=banks[:, bank, :],
                                           scalar=-float(HD) ** -0.5 if u == 0 else 1.0, in1=rstd[:, cols],
                                           op0=ALU.mult, op1=ALU.mult).then_inc(t_ready, 1)

        def aug_act(act, p, h, idx):
            u, n = UNIT_HALF[idx]
            cols = slice(n * BANK, (n + 1) * BANK)
            rows = slice(h * HD, (h + 1) * HD)
            act.wait_ge(t_ready, 6 * p + idx + 1)
            parts, ext = (q_parts, q_ext) if u == 0 else (k_parts, k_ext)
            own = slice(HD, P) if u == 0 else slice(0, HD)
            nc.scalar.activation(ext[rows, h, cols], t[rows, u, cols], ACT.Copy).then_inc(aug_hi_ready[h], 1)
            nc.scalar.activation(parts[own, h, cols], t[rows, u, cols], ACT.Copy).then_inc(aug_hi_ready[h], 1)

        def aug_dve(dve, p, h, idx):
            u, n = UNIT_HALF[idx]
            cols = slice(n * BANK, (n + 1) * BANK)
            rows = slice(h * HD, (h + 1) * HD)
            parts, ext = (q_parts, q_ext) if u == 0 else (k_parts, k_ext)
            own = slice(0, HD) if u == 0 else slice(HD, P)
            dve.wait_ge(aug_hi_ready[h], 8 * p + 2 * idx + 2)
            nc.vector.tensor_tensor(parts[own, h, cols], t[rows, u, cols], ext[rows, h, cols].bitcast(F32),
                                    ALU.subtract).then_inc(aug_ready[h], 1)

        def probs(h, b):
            return p_low[:, b, 0:(b + 1) * P] if b < 4 else p_high[:, b - 4, 0:(b + 1) * P]

        def scores(s):
            b = s % 8
            return banks[:, 2 * (s % 2):2 * (s % 2) + 2, :].rearrange("p a n -> p (a n)")[:, 0:(b + 1) * P]

        def first_col(g, j):
            return max(0, j - 4 * g) * P

        def attend_pe(pe, p, proj):
            for s in range(STEPS_A):
                if s < 16:
                    h, b = divmod(s, 8)
                    if b % 4 == 0:
                        pe.wait_ge(aug_ready[h], 4 * p + 2 + b // 2)
                    if b == 0:
                        pe.wait_ge(ext_loaded[h], 32 * (p + 1))
                    if s >= 2:
                        pe.wait_ge(exp_ready, 16 * p + s - 1)
                    width = (b + 1) * P
                    qs = slice(b * P, (b + 1) * P)
                    rows = slice(0, HD + 4) if h == 0 else slice(0, P)
                    for c0 in range(0, width, BANK):
                        c1 = min(width, c0 + BANK)
                        psum = banks[:, 2 * (s % 2) + c0 // BANK, 0:c1 - c0]
                        diagonal = c1 == width
                        nc.tensor.matmul(psum, q_parts[:, h, qs], k_parts[:, h, c0:c1], start=True, stop=False)
                        mm = nc.tensor.matmul(psum, q_ext[rows, h, qs], k_ext[rows, h, c0:c1],
                                              start=False, stop=not diagonal)
                        if diagonal:
                            mm = nc.tensor.matmul(banks[:, 2 * (s % 2) + c0 // BANK, c1 - c0 - P:c1 - c0],
                                                  ident_r[:], mask[:], start=False, stop=True)
                    mm.then_inc(scores_done, 1)
                v_steps = V_STEPS if proj else V_STEPS_LAST
                if s in v_steps:
                    i = v_steps.index(s)
                    if i == 0:
                        pe.wait_ge(t_ready, 6 * p + 4)
                    elif i == 3:
                        pe.wait_ge(o_ready, 4 * p + 1)
                    project_pe(pe, p, 4 + i // 3, i % 3, 7 - i // 3)
                if proj and s in QK_STEPS:
                    i = QK_STEPS.index(s)
                    if i % 3 == 0:
                        pe.wait_ge(t_ready, 6 * (p + 1) + (i // 3 if i else -1))
                    project_pe(pe, p + 1, i // 3, i % 3, 7)
                if not proj and s in FILL_AT:
                    fill_pe(pe, *FILL_AT[s])
                for r in TURNS_AT.get(s - 2, ()):
                    h, g, j = TURNS[r]
                    if h == "v":
                        continue
                    pe.wait_ge(part_ready, len(TURNS) * p + r + 1)
                    if j == 0:
                        pe.wait_ge(o_ready, 4 * p + 2 * h + g + 1)
                        if h == 0 and g == 0:
                            pe.wait_ge(t_ready, 6 * p + 6)
                    c0 = first_col(g, j)
                    nc.tensor.matmul(banks[:, 6, c0:BANK], v_parts[:, j, h, :, :], pt_hi[:, r % 4, c0:BANK],
                                     start=j == 0, stop=False)
                    nc.tensor.matmul(banks[:, 6, c0:BANK], v_parts[:, j, h, :, :], pt_lo[:, r % 4, c0:BANK],
                                     start=False, stop=j == 4 * g + 3).then_inc(pv_done, 1)
                for r in TURNS_AT.get(s, ()):
                    h, g, j = TURNS[r]
                    if r >= 2:
                        pe.wait_ge(part_ready, len(TURNS) * p + r - 1)
                    if h == "v":
                        pe.wait_ge(t_ready, 6 * p + 5 + g)
                        for i in range(4):
                            mm = nc.tensor.transpose(banks[:, 4 + r % 2, i * P:(i + 1) * P],
                                                     t[:, 2, g * BANK + i * P:g * BANK + (i + 1) * P], ident[:])
                    else:
                        if j == 0:
                            pe.wait_ge(p_ready, 16 * p + 8 * h + 4 * g + 4)
                        for i in range(first_col(g, j) // P, 4):
                            src = (p_high if g else p_low)[:, i, j * P:(j + 1) * P]
                            mm = nc.tensor.transpose(banks[:, 4 + r % 2, i * P:(i + 1) * P], src, ident[:])
                    mm.then_inc(turned, 1)

        def o_half_act(act, p, i):
            act.wait_ge(pv_done, 24 * p + (4, 12, 16, 24)[i])
            act.wait_ge(o_ready, 4 * p + i + 1)
            nc.scalar.activation(o_half[0:HD, :], banks[HD:P, 6, :], ACT.Copy).then_inc(o_half_ready, 1)

        def o_dve(dve, p, i):
            h, g = divmod(i, 2)
            if i == 0:
                dve.wait_ge(oT_free, 16 * (p + 1))
            dve.wait_ge(o_half_ready, 4 * p + i + 1)
            nc.vector.tensor_tensor(oT[h * HD:(h + 1) * HD, g * BANK:(g + 1) * BANK], banks[0:HD, 6, :],
                                    o_half[0:HD, :], ALU.add).then_inc(o_ready, 1)

        def o7_act(act, n):
            cols = slice(n * BANK, (n + 1) * BANK)
            act.wait_ge(o_ready, 4 * (PAIRS - 1) + 4 + n)
            nc.scalar.activation(hn_hi[:, KT - 1, cols], oT[:, cols], ACT.Copy).then_inc(o7_hi_ready, 1)

        def o7_dve(dve, n):
            cols = slice(n * BANK, (n + 1) * BANK)
            dve.wait_ge(o7_hi_ready, n + 1)
            nc.vector.tensor_tensor(hn_lo[:, KT - 1, cols], oT[:, cols], hn_hi[:, KT - 1, cols].bitcast(F32),
                                    ALU.subtract).then_inc(o7_ready, 1)

        def attend_act(act, p, proj):
            for s in range(STEPS_A):
                for r in TURNS_AT.get(s - 1, ()):
                    h, g, j = TURNS[r]
                    act.wait_ge(turned, len(TURNS) * p + r + 1)
                    if h == "v":
                        nc.scalar.activation(v_parts[:, 4 * g:4 * g + 4, :, 0, :],
                                             banks[:, 4 + r % 2, :].rearrange("p (j h d) -> p j h d", j=4, h=2),
                                             ACT.Copy).then_inc(part_hi_ready, 1)
                    else:
                        c0 = first_col(g, j)
                        nc.scalar.activation(pt_hi[:, r % 4, c0:BANK], banks[:, 4 + r % 2, c0:BANK],
                                             ACT.Copy).then_inc(part_hi_ready, 1)
                if s - 1 in O_AT:
                    o_half_act(act, p, O_AT[s - 1])
                if s == 0:
                    aug_act(act, p, 0, 3)
                if s in SLOT1_AT:
                    aug_act(act, p, 1, SLOT1_AT[s])
                if proj and s in SLOT0_AT:
                    aug_act(act, p + 1, 0, SLOT0_AT[s])
                if not proj and s in TAIL_AT:
                    tail_act(act, TAIL_AT[s])
                if s < 16:
                    if s == 12:
                        act.wait_ge(turned, len(TURNS) * p + 14)
                    act.wait_ge(low_ready, 16 * p + s + 1)
                    nc.scalar.activation(probs(s // 8, s % 8), scores(s), ACT.Exp, bias=low[:, s:s + 1], scale=-1.0,
                                         accum_out=rsum[:, s:s + 1]).then_inc(exp_ready, 1)
                if proj and s in W_AT:
                    pw_split_act(act, p + 1, W_AT[s])
                if not proj and s == O7_AT:
                    o7_act(act, 0)
            o_half_act(act, p, 3)

        def attend_dve(dve, p, proj):
            for s in range(STEPS_A):
                for r in TURNS_AT.get(s - 1, ()):
                    h, g, j = TURNS[r]
                    dve.wait_ge(part_hi_ready, len(TURNS) * p + r + 1)
                    if h == "v":
                        for head in range(2):
                            v = nc.vector.tensor_tensor(
                                v_parts[:, 4 * g:4 * g + 4, head, 1, :],
                                banks[:, 4 + r % 2, :].rearrange("p (j h d) -> p j h d", j=4, h=2)[:, :, head, :],
                                v_parts[:, 4 * g:4 * g + 4, head, 0, :].bitcast(F32), ALU.subtract)
                        v.then_inc(part_ready, 1)
                    else:
                        c0 = first_col(g, j)
                        nc.vector.tensor_tensor(pt_lo[:, r % 4, c0:BANK], banks[:, 4 + r % 2, c0:BANK],
                                                pt_hi[:, r % 4, c0:BANK].bitcast(F32),
                                                ALU.subtract).then_inc(part_ready, 1)
                if s < 16:
                    dve.wait_ge(scores_done, 16 * p + s + 1)
                    nc.vector.tensor_reduce(low[:, s:s + 1], scores(s), AX_X, ALU.min).then_inc(low_ready, 1)
                if s - 1 in O_AT:
                    o_dve(dve, p, O_AT[s - 1])
                if 1 <= s <= 16:
                    dve.wait_ge(exp_ready, 16 * p + s)
                    nc.vector.reciprocal(rinv[:, s - 1:s], rsum[:, s - 1:s]).then_inc(rinv_ready, 1)
                    dve.wait_ge(rinv_ready, 16 * p + s)
                    pr = probs((s - 1) // 8, (s - 1) % 8)
                    nc.vector.tensor_scalar(pr, pr, rinv[:, s - 1:s], None, ALU.mult).then_inc(p_ready, 1)
                if s == 0:
                    aug_dve(dve, p, 0, 3)
                if s in SLOT1_AT:
                    aug_dve(dve, p, 1, SLOT1_AT[s])
                if proj and s in SLOT0_AT:
                    aug_dve(dve, p + 1, 0, SLOT0_AT[s])
                v_steps = V_STEPS if proj else V_STEPS_LAST
                if s in v_steps[2::3]:
                    t_dve(dve, p, 4 + v_steps.index(s) // 3, 7 - v_steps.index(s) // 3)
                if proj and s in QK_STEPS[2::3]:
                    t_dve(dve, p + 1, QK_STEPS.index(s) // 3, 7)
                if not proj and s == O7_AT:
                    o7_dve(dve, 0)
            o_dve(dve, p, 3)

        def attend_pool(pool, p, proj):
            for s in range(STEPS_A):
                if not proj and s in TAIL_AT:
                    tail_low(pool, nc.gpsimd, TAIL_AT[s])
                if proj and s in W_AT:
                    pw_split_low(pool, nc.gpsimd, p + 1, W_AT[s])
                if proj and s % 8 == 7:
                    pool.wait_ge(scores_done, 16 * p + s + 1)
                    ext_load(pool, p + 1, s // 8)
            if proj:
                pool.wait_ge(o_ready, 4 * (p + 1) + 1)
                pool.dma_start(o_dram[bass.ds(p, 1), :, :].rearrange("a p s -> (a p) s"), oT[:]).then_inc(oT_free, 16)

        def ext_load(pool, p, h):
            r = HD if h == 0 else 0
            for dst in (k_ext[r:r + 2, h, :], q_ext[r + 2:r + 4, h, :]):
                pool.dma_start(dst, ext_dram[bass.ds(2 * p + h, 1), :, :].rearrange("h a s -> (h a) s")
                               ).then_inc(ext_loaded[h], 16)

        def tail_place(e):
            if 1 <= e < KT:
                return hn_hi[:, e - 1, :], hn_lo[:, e - 1, :]
            return wo_unit(tail_unit(e))

        def tail_unit(e):
            return 0 if e == 0 else e - (KT - 1)

        def tail_unit_ready(m):
            return 1 if m == 0 else KT + m

        def wo_unit(m):
            return (wa_hi[:, m, :], wa_lo[:, m, :]) if m < 3 else (wo_hi[:, m - 3, :], wo_lo[:, m - 3, :])

        def tail_sync(sp):
            for e in range(TAIL):
                if e < RAW:
                    sp.wait_ge(pw_ready[e], PAIRS)
                else:
                    sp.wait_ge(tail_ready, e - RAW + 1)
                slot = raw[:, e % RAW, :]
                if 1 <= e < KT:
                    sp.wait_ge(oT_free, 16 * (e + 1))
                    sp.dma_start(slot, o_dram[e - 1]).then_inc(tail_loaded[e % RAW], 16)
                else:
                    m = tail_unit(e)
                    sp.dma_start(slot.rearrange("p (k n) -> p k n", n=P),
                                 fox_w_o[0, :, m * P:(m + 1) * P].rearrange("(k p) n -> p k n", p=P)
                                 ).then_inc(tail_loaded[e % RAW], 16)

        def tail_act(act, e):
            act.wait_ge(tail_loaded[e % RAW], 16 * (e // RAW + 1))
            nc.scalar.activation(tail_place(e)[0], raw[:, e % RAW, :], ACT.Copy).then_inc(tail_hi_ready, 1)

        def tail_low(eng, ops, e):
            eng.wait_ge(tail_hi_ready, e + 1)
            hi, lo = tail_place(e)
            ops.tensor_tensor(lo, raw[:, e % RAW, :], hi.bitcast(F32), ALU.subtract).then_inc(tail_ready, 1)

        def wo_piece_pe(j, k):
            n, m = divmod(j, KT)
            cols = slice(n * BANK, (n + 1) * BANK)
            w = slice(k * P, (k + 1) * P)
            hi, lo = wo_unit(m)
            return three(banks[:, WO_BANK[j], :], hi[:, w], lo[:, w], hn_hi[:, k, cols], hn_lo[:, k, cols],
                         k == 0, k == KT - 1)

        def fill_pe(pe, j, k0, k1):
            if j == 0:
                pe.wait_ge(tail_ready, k1 + 1)
            elif k0 == 0:
                pe.wait_ge(tail_ready, max(KT, tail_unit_ready(j % KT)))
                pe.wait_ge(exp_ready, 16 * PAIRS)
            for k in range(k0, k1):
                wo_piece_pe(j, k)

        def wo_pe(pe):
            for j in range(OUTS):
                n, m = divmod(j, KT)
                if n == 0:
                    pe.wait_ge(tail_ready, tail_unit_ready(m))
                earlier = [i for i in range(j) if WO_BANK[i] == WO_BANK[j]]
                if earlier:
                    pe.wait_ge(wo_added, earlier[-1] + 1)
                for k in range(KT - 1 if j in STARTED else 0, KT):
                    if j % KT == 0 and k == KT - 1:
                        pe.wait_ge(o7_ready, n + 1)
                    mm = wo_piece_pe(j, k)
                mm.then_inc(wo_done, 1)

        block = ctx.enter_context(nc.Block())

        @block.sync
        def _(sp):
            sp.dma_start(gain_rows[0:KT, :], norm_ffn1[0, :].rearrange("(k p) -> k p", p=P)).then_inc(gains_loaded, 16)
            for b in range(SB):
                sp.dma_start(xin[:, b, :], x[0, b * P:(b + 1) * P, :]).then_inc(x_loaded[b], 16)
                if b == 3:
                    for u in range(RAW):
                        ffn_load(sp, ffn1, 0, u)
                if b == 5:
                    sp.wait_ge(w_ready[0], 1)
                    ffn_load(sp, ffn1, 0, RAW)
            ffn_sync(sp, ffn1, RAW + 1)
            for u in range(RAW):
                sp.wait_ge(w_ready[u + RAW], CHUNKS)
                pair_load(sp, 0, u)
            for kt in range(KT):
                sp.wait_ge(x_updated, OUTS * (CHUNKS - 1) + KT + kt + 1)
                sp.dma_start(x_dram[kt], xT[:, kt, :]).then_inc(x_spilled, 16)
            with sp.Fori(0, PAIRS - 1) as p:
                for u in range(3):
                    sp.wait_ge(pw_ready[u], p + 1)
                    pair_load(sp, p + 1, u)
            tail_sync(sp)
            for u in range(RAW):
                sp.wait_ge(tail_ready, TAIL - RAW + u + 1)
                ffn_load(sp, ffn2, CHUNKS, u)
            ffn_sync(sp, ffn2)
            for b in range(SB):
                sp.wait_ge(yout_act, b + 1)
                sp.wait_ge(yout_dve, b + 1)
                sp.dma_start(out[0, b * P:(b + 1) * P, :], yout[:, b, :]).then_inc(stored, 16)
            sp.wait_ge(stored, 16 * SB)

        @block.gpsimd
        def _(pool):
            nc.gpsimd.memset(ident[:], 0.0).then_inc(ident_made, 1)
            pool.wait_ge(ident_made, 1)
            nc.gpsimd.affine_select(out=ident[:], in_=ident[:], compare_op=ALU.not_equal, fill=1.0, base=0,
                                    pattern=[[-1, P]], channel_multiplier=1).then_inc(ident_made, 1)
            pool.dma_start(b_f[:], fox_b_f.rearrange("a h -> h a")).then_inc(gate_in_loaded, 16)
            pool.dma_start(wf_raw[:], fox_w_in[0, :, 3 * D:3 * D + NH].rearrange("(k p) n -> p k n", p=P)
                           ).then_inc(gate_in_loaded, 16)
            nc.gpsimd.memset(mask0[:], 0.0).then_inc(mask_made, 1)
            pool.wait_ge(mask_made, 1)
            nc.gpsimd.affine_select(out=mask0[:], in_=mask0[:], compare_op=ALU.is_ge, fill=1e38, base=0,
                                    pattern=[[-1, P]], channel_multiplier=1).then_inc(mask_made, 1)
            pool.wait_ge(w_hi_ready[2], 1)
            nc.gpsimd.tensor_tensor(wlo(2), raw[:, 2, :], whi(2).bitcast(F32), ALU.subtract).then_inc(w_ready[2], 1)
            norm_pool(pool, norm2)
            pool.wait_ge(x_spilled, 16 * KT)
            pool.wait_ge(hn_ready, norm2.tiles + NS * KT)
            for ext in (k_ext, q_ext):
                nc.gpsimd.memset(ext[0:HD, 1, :].bitcast(F32), 0.0).then_inc(rows_zero, 1)
            pool.wait_ge(rows_zero, 2)
            for ext, one in ((k_ext, -1.0), (q_ext, 1.0)):
                nc.gpsimd.memset(ext[HD:HD + 4, 0, :].bitcast(F32), one).then_inc(rows_one, 1)
                nc.gpsimd.memset(ext[0:4, 1, :].bitcast(F32), one).then_inc(rows_one, 1)
            pool.wait_ge(f_act, 4)
            pool.wait_ge(f_step, 6)
            pool.dma_start(ext_dram, ext_rows[:]).then_inc(oT_free, 16)
            pool.wait_ge(oT_free, 16)
            pool.wait_ge(rows_one, 4)
            for h in range(2):
                ext_load(pool, 0, h)
            with pool.Fori(0, PAIRS - 1) as p:
                attend_pool(pool, p, True)
            attend_pool(pool, PAIRS - 1, False)
            pool.wait_ge(scores_done, 16 * PAIRS)
            for kt in range(KT):
                pool.dma_start(xT[:, kt, :], x_dram[kt]).then_inc(x_back[kt], 16)
            norm_pool(pool, norm3)
            norm_pool(pool, normf)

        @block.tensor
        def _(pe):
            pe.wait_ge(ident_made, 2)
            for b in range(4):
                x_turn_pe(pe, b)
                if b == 2:
                    pe.wait_ge(gains_loaded, 64)
                    pe.wait_ge(x_kept_act, 1)
                    nc.tensor.transpose(banks[:, 0, 0:4 * KT], gain_rows[:],
                                        ident[0:4 * KT, 0:4 * KT]).then_inc(gains_turned, 1)
            pe.wait_ge(ones_made, 1)
            ffn_pe(pe, ffn1, norm1, 0, first=True)
            with pe.Fori(1, CHUNKS) as c:
                ffn_pe(pe, ffn1, norm1, c)
            pe.wait_ge(wf_ready, 1)
            pe.wait_ge(x_updated, OUTS * CHUNKS)
            stat_pe(pe, norm2, 0, 4)
            for n in range(NS):
                cols = slice(n * BANK, (n + 1) * BANK)
                for k in range(KT):
                    pe.wait_ge(hn_ready, norm2.tiles + n * KT + k + 1)
                    mm = three(banks[0:NH, 6 + n, :], wf_hi[:, k, :], wf_lo[:, k, :], hn_hi[:, k, cols],
                               hn_lo[:, k, cols], k == 0, k == KT - 1)
                mm.then_inc(f_done, 1)
            stat_pe(pe, norm2, 1, 5)
            rstd_pe(pe, norm2, 0)
            for idx in range(4):
                for part in range(3):
                    project_pe(pe, 0, idx, part, idx)
                    if (idx, part) == (0, 0):
                        rstd_pe(pe, norm2, 1)
            pe.wait_ge(ident_r_made, 2)
            with pe.Fori(0, PAIRS - 1) as p:
                attend_pe(pe, p, True)
            attend_pe(pe, PAIRS - 1, False)
            wo_pe(pe)
            ffn_pe(pe, ffn2, norm3, CHUNKS, first=True)
            with pe.Fori(CHUNKS + 1, 2 * CHUNKS - 1) as c:
                ffn_pe(pe, ffn2, norm3, c)
            ffn_pe(pe, ffn2, norm3, 2 * CHUNKS - 1, last=True)
            for b in range(5, SB):
                y_turn_pe(pe, b)

        @block.scalar
        def _(act):
            for i, g in ((1, norm_mix[0, :]), (2, norm_ffn2[0, :]), (3, norm_final)):
                act.dma_start(gain_rows[i * KT:(i + 1) * KT, :],
                              g.rearrange("(k p) -> k p", p=P)).then_inc(gains_loaded, 16)

            def keep_act(b):
                act.wait_ge(x_turned, 2 * b + 1)
                bank = 2 * b if b < 4 else 4 + 2 * (b % 2)
                nc.scalar.activation(xT[:, 0:4, b * P:(b + 1) * P],
                                     banks[:, bank, :].rearrange("p (k s) -> p k s", k=4),
                                     ACT.Copy).then_inc(x_kept_act, 1)

            def x_square_act(b):
                act.wait_ge(x_loaded[b], 16)
                if b:
                    act.wait_ge(x_squared, b)
                nc.scalar.activation(sq[:].rearrange("p a n -> p (a n)"), xin[:, b, :], ACT.Square,
                                     accum_out=rstd_col[:, b:b + 1]).then_inc(x_squared, 1)

            for b in range(4):
                if b < 3:
                    x_square_act(b)
                else:
                    w_split_act(act, ffn1, 0, 0)
                keep_act(b)
            act.wait_ge(gains_ready, 1)
            act.wait_ge(x_kept_act, 4)
            act.wait_ge(x_kept_dve, 4)
            for j in range(KT):
                norm_act(norm1, j)
                if j == 2:
                    w_split_act(act, ffn1, 0, 1)
            w_split_act(act, ffn1, 0, 2)
            x_square_act(3)
            keep_act(4)
            keep_act(5)
            w_split_act(act, ffn1, 0, 3)
            x_square_act(4)
            keep_act(6)
            x_square_act(5)
            keep_act(7)
            act.wait_ge(x_kept_act, SB)
            act.wait_ge(x_kept_dve, SB)
            for j in range(KT, NS * KT):
                norm_act(norm1, j)
            x_square_act(6)
            x_square_act(7)
            for n in range(NS):
                rcol_act(act, norm1, n)
            ffn_act(act, ffn1, norm1, 0, first=True)
            with act.Fori(1, CHUNKS - 1) as c:
                ffn_act(act, ffn1, norm1, c)
            act.wait_ge(gate_in_loaded, 32)
            nc.scalar.activation(wf_hi[:], wf_raw[:], ACT.Copy).then_inc(wf_hi_ready, 1)
            ffn_act(act, ffn1, norm1, CHUNKS - 1, last=True)
            act.wait_ge(up_done, STEPS * CHUNKS)
            for u in range(3):
                pw_split_act(act, 0, u)
            for j in range(NS * KT):
                act.wait_ge(x_updated, OUTS * (CHUNKS - 1) + j + 1)
                norm_act(norm2, j)
                square_act(act, norm2, j)
            for n in range(NS):
                rstd_act(act, norm2, n)
            act.wait_ge(f_step, 3)
            nc.scalar.activation(ez[:], z[:], ACT.Abs).then_inc(f_act, 1)
            act.wait_ge(f_act, 1)
            nc.scalar.activation(ez[:], ez[:], ACT.Exp, scale=-1.0).then_inc(f_act, 1)
            act.wait_ge(f_act, 2)
            nc.scalar.activation(ez[:], ez[:], ACT.Ln, bias=1.0).then_inc(f_act, 1)
            act.wait_ge(x_spilled, 16 * KT)
            aug_act(act, 0, 0, 0)
            act.wait_ge(f_step, 5)
            nc.scalar.activation(ext_rows[:, 0, :], cum[:], ACT.Copy).then_inc(f_act, 1)
            for idx in (1, 2):
                aug_act(act, 0, 0, idx)
            with act.Fori(0, PAIRS - 1) as p:
                attend_act(act, p, True)
            attend_act(act, PAIRS - 1, False)
            o7_act(act, 1)
            for e in range(len(TAIL_AT), TAIL):
                tail_act(act, e)
            for j in range(NS * KT):
                if j % KT == 0:
                    act.wait_ge(wo_done, KT * (j // KT + 1))
                    if j:
                        w_split_act(act, ffn2, CHUNKS, 3)
                act.wait_ge(wo_added, j + 1)
                norm_act(norm3, j)
                square_act(act, norm3, j)
                if j == KT - 1:
                    act.wait_ge(wo_done, KT + 3)
                    for u in range(3):
                        w_split_act(act, ffn2, CHUNKS, u)
            ffn_act(act, ffn2, norm3, CHUNKS, first=True)
            with act.Fori(CHUNKS + 1, 2 * CHUNKS - 1) as c:
                ffn_act(act, ffn2, norm3, c)
            ffn_act(act, ffn2, norm3, 2 * CHUNKS - 1, last=True)
            act.wait_ge(up_done, STEPS * 2 * CHUNKS)
            for j in range(NS * KT):
                act.wait_ge(x_updated, OUTS * (2 * CHUNKS - 1) + j + 1)
                square_act(act, normf, j)
                y_act(act, j)
                if j == Y_FIRST:
                    rcol_act(act, normf, 0)
                if j in (Y_FIRST + 1, Y_FIRST + 3):
                    for b in range(j - Y_FIRST - 1, j - Y_FIRST + 1):
                        yout_block_act(act, b)
            rcol_act(act, normf, 1)
            for b in range(4, SB):
                yout_block_act(act, b)

        @block.vector
        def _(dve):
            nc.vector.memset(ones[:].bitcast(F32), 1.0).then_inc(ones_made, 1)
            dve.wait_ge(ident_made, 2)
            nc.vector.tensor_copy(ident_r[:], ident[:]).then_inc(ident_r_made, 1)
            dve.wait_ge(mask_made, 2)
            nc.vector.tensor_copy(mask[:], mask0[:]).then_inc(ident_r_made, 1)
            def keep_dve(b):
                dve.wait_ge(x_turned, 2 * b + 2)
                bank = 2 * b + 1 if b < 4 else 5 + 2 * (b % 2)
                nc.vector.tensor_copy(xT[:, 4:8, b * P:(b + 1) * P],
                                      banks[:, bank, :].rearrange("p (k s) -> p k s", k=4)
                                      ).then_inc(x_kept_dve, 1)

            for b in range(4):
                if b == 3:
                    dve.wait_ge(gains_turned, 1)
                    nc.vector.tensor_copy(gains[:], banks[:, 0, 0:4 * KT]).then_inc(gains_ready, 1)
                keep_dve(b)
            w_split_dve(dve, ffn1, 0, 0)
            dve.wait_ge(gains_ready, 1)
            for j in range(KT):
                norm_dve(dve, norm1, j)
                if j == 2:
                    w_split_dve(dve, ffn1, 0, 1)
            keep_dve(4)
            keep_dve(5)
            w_split_dve(dve, ffn1, 0, 3)
            keep_dve(6)
            keep_dve(7)
            for j in range(KT, NS * KT):
                norm_dve(dve, norm1, j)
            for n in range(NS):
                rcol_dve(dve, norm1, n, None)
            ffn_dve(dve, ffn1, norm1, 0, first=True)
            with dve.Fori(1, CHUNKS - 1) as c:
                ffn_dve(dve, ffn1, norm1, c)
            dve.wait_ge(wf_hi_ready, 1)
            nc.vector.tensor_tensor(wf_lo[:], wf_raw[:], wf_hi[:].bitcast(F32), ALU.subtract).then_inc(wf_ready, 1)
            ffn_dve(dve, ffn1, norm1, CHUNKS - 1, last=True)
            norm_dve(dve, norm2, KT)
            norm_dve(dve, norm2, KT + 1)
            rcol_dve(dve, norm2, 0, 4)
            for j in range(KT + 2, NS * KT):
                norm_dve(dve, norm2, j)
            rcol_dve(dve, norm2, 1, 5)

            def z_dve(n):
                cols = slice(n * BANK, (n + 1) * BANK)
                dve.wait_ge(f_done, n + 1)
                dve.wait_ge(rstd_ready, norm2.halves + n + 1)
                nc.vector.tensor_tensor(z[:, cols], banks[0:NH, 6 + n, :], rstd[0:NH, cols],
                                        ALU.mult).then_inc(f_step, 1)

            z_dve(0)
            z_dve(1)
            dve.wait_ge(f_step, 2)
            nc.vector.tensor_scalar(z[:], z[:], b_f[:], None, ALU.add).then_inc(f_step, 1)
            t_dve(dve, 0, 0, 0)
            dve.wait_ge(f_act, 3)
            nc.vector.scalar_tensor_tensor(out=z[:], in0=z[:], scalar=0.0, in1=ez[:], op0=ALU.min,
                                           op1=ALU.subtract).then_inc(f_step, 1)
            dve.wait_ge(f_step, 4)
            nc.vector.tensor_tensor_scan(cum[:], ones[0:NH, 0:1].bitcast(F32).to_broadcast([NH, S]), z[:], 0.0,
                                         ALU.mult, ALU.add).then_inc(f_step, 1)
            dve.wait_ge(f_step, 5)
            dve.wait_ge(f_act, 4)
            nc.vector.tensor_tensor(ext_rows[:, 1, :], cum[:], ext_rows[:, 0, :].bitcast(F32),
                                    ALU.subtract).then_inc(f_step, 1)
            t_dve(dve, 0, 1, 1)
            dve.wait_ge(x_spilled, 16 * KT)
            aug_dve(dve, 0, 0, 0)
            aug_dve(dve, 0, 0, 1)
            t_dve(dve, 0, 2, 2)
            aug_dve(dve, 0, 0, 2)
            t_dve(dve, 0, 3, 3)
            nc.vector.tensor_copy(rinv[:], rstd[:, 0:16]).then_inc(o_ready, 1)
            with dve.Fori(0, PAIRS - 1) as p:
                attend_dve(dve, p, True)
            attend_dve(dve, PAIRS - 1, False)
            o7_dve(dve, 1)
            dve.wait_ge(tail_ready, len(TAIL_AT))
            for e in range(len(TAIL_AT), TAIL):
                tail_low(dve, nc.vector, e)
            for j in range(NS * KT):
                m, cols = halves(j)
                dve.wait_ge(wo_done, j + 1)
                if j < KT:
                    dve.wait_ge(x_back[j], 16)
                nc.vector.tensor_tensor(xT[:, m, cols], banks[:, WO_BANK[j], :], xT[:, m, cols],
                                        ALU.add).then_inc(wo_added, 1)
                if j >= KT:
                    norm_dve(dve, norm3, j - KT)
                if 12 <= j < 15:
                    w_split_dve(dve, ffn2, CHUNKS, j - 12)
            w_split_dve(dve, ffn2, CHUNKS, 3)
            for j in range(KT, NS * KT):
                norm_dve(dve, norm3, j)
            ffn_dve(dve, ffn2, norm3, CHUNKS, first=True)
            with dve.Fori(CHUNKS + 1, 2 * CHUNKS - 1) as c:
                ffn_dve(dve, ffn2, norm3, c)
            ffn_dve(dve, ffn2, norm3, 2 * CHUNKS - 1, last=True)
            rcol_dve(dve, normf, 1, Y_BANK[1])
            for b in range(4, SB):
                yout_block_dve(dve, b)


_INS = ["x", "norm_ffn1", "norm_mix", "norm_ffn2", "norm_final",
        "ffn1_w_gate", "ffn1_w_up", "ffn1_w_down", "ffn2_w_gate", "ffn2_w_up", "ffn2_w_down",
        "fox_w_in", "fox_b_f", "fox_w_o"]


def kernel(**inputs):
    import numpy as _np
    import concourse.bacc as _bacc
    from concourse import mybir as _mybir
    from concourse.bass_utils import run_bass_kernel_spmd as _run

    nc = _bacc.Bacc("TRN2", target_bir_lowering=False, num_devices=1)
    arrays, args = {}, []
    for name in _INS:
        a = _np.ascontiguousarray(inputs[name])
        arrays[f"in_{name}_dram"] = a
        args.append(nc.dram_tensor(f"in_{name}_dram", a.shape, _mybir.dt.from_np(a.dtype), kind="ExternalInput").ap())
    shape = arrays["in_x_dram"].shape
    args.append(nc.dram_tensor("out_dram", shape, _mybir.dt.float32, kind="ExternalOutput").ap())
    build(nc, *args)
    r = _run(nc, [arrays], core_ids=[0])
    return r.results[0]["out_dram"]
```
